# Optimizing a Trainium2 kernel written in Bass

```python
import math
import jax, jax.numpy as jnp
from jax import lax
import numpy as np

D_MODEL = 1024
BATCH = 1
SEQ = 256
DEPTH = 2

HG_HEADS = 4
HG_DIM = 128
HG_WIDTH = HG_HEADS * HG_DIM
HG_CHUNK = 64
AT_HEADS = 4
AT_DIM = 64
AT_WIDTH = AT_HEADS * AT_DIM
MOBA_BLOCK = 256
MOBA_TOPK = 3
MOBA_QBLOCK = 64
REL_BUCKETS = 32
REL_MAX_DIST = 1024
CV_GROUPS = 4
CV_WIDTH = CV_GROUPS * 64
CV_KERNEL = 3
D_MIX = HG_WIDTH + AT_WIDTH + CV_WIDTH
D_IN = 4 * HG_WIDTH + 3 * AT_WIDTH + 3 * CV_WIDTH
D_FF = 2816
EPS = 1e-6

kernel_name = 'hybrid_hgrn2_moba_shortconv'

def rms_norm(x, w):
    xf = x.astype(jnp.float32)
    y = xf * lax.rsqrt(jnp.mean(xf * xf, axis=-1, keepdims=True) + EPS)
    return (y * w.astype(jnp.float32)).astype(x.dtype)

def swiglu(x, wg, wu, wd):
    return (jax.nn.silu(x @ wg) * (x @ wu)) @ wd

def t5_bucket(dist):
    dist = jnp.maximum(dist, 0)
    max_exact = REL_BUCKETS // 2
    d = jnp.maximum(dist, 1).astype(jnp.float32)
    large = max_exact + (jnp.log(d / max_exact) / math.log(REL_MAX_DIST / max_exact)
                         * (REL_BUCKETS - max_exact)).astype(jnp.int32)
    large = jnp.minimum(large, REL_BUCKETS - 1)
    return jnp.where(dist < max_exact, dist, large)

def hgrn2_mixer(q, f_pre, i, g, lb, norm_w):
    B, S, _ = q.shape
    f32 = jnp.float32
    nc = S // HG_CHUNK
    fp = f_pre.astype(f32)
    lbf = lb.astype(f32)
    log_f = jnp.log(lbf + (1.0 - lbf) * jax.nn.sigmoid(fp))
    k = (1.0 - lbf) * jax.nn.sigmoid(-fp)

    def to_chunks(t):
        return t.astype(f32).reshape(B, nc, HG_CHUNK, HG_HEADS, HG_DIM).transpose(1, 0, 3, 2, 4)

    qc, kc, vc, lc = to_chunks(q), to_chunks(k), to_chunks(i), to_chunks(log_f)
    causal = jnp.tril(jnp.ones((HG_CHUNK, HG_CHUNK), dtype=bool))

    def step(state, xs):
        qt, kt, vt, lt = xs
        b = jnp.cumsum(lt, axis=2)
        diff = b[:, :, :, None, :] - b[:, :, None, :, :]
        decay = jnp.exp(jnp.where(causal[:, :, None], diff, -jnp.inf))
        scores = jnp.einsum('bhtk,bhsk,bhtsk->bhts', qt, kt, decay)
        o = (jnp.einsum('bhts,bhsv->bhtv', scores, vt)
             + jnp.einsum('bhtk,bhkv->bhtv', qt * jnp.exp(b), state))
        b_last = b[:, :, -1:, :]
        new_state = (jnp.exp(b_last[:, :, 0, :, None]) * state
                     + jnp.einsum('bhsk,bhsv->bhkv', kt * jnp.exp(b_last - b), vt))
        return new_state, o

    s0 = jnp.zeros((B, HG_HEADS, HG_DIM, HG_DIM), f32)
    _, o = lax.scan(step, s0, (qc, kc, vc, lc))
    o = o.transpose(1, 0, 3, 2, 4).reshape(B, S, HG_HEADS, HG_DIM)
    gate = jax.nn.silu(g.astype(f32).reshape(B, S, HG_HEADS, HG_DIM))
    o = rms_norm(o, norm_w) * gate
    return o.reshape(B, S, HG_WIDTH)

def moba_mixer(q, k, v, rel_bias):
    B, S, _ = q.shape
    f32 = jnp.float32
    nblk = -(-S // MOBA_BLOCK)
    s_pad = nblk * MOBA_BLOCK
    pad = ((0, 0), (0, s_pad - S), (0, 0))

    def heads(t):
        return jnp.pad(t.astype(f32), pad).reshape(B, s_pad, AT_HEADS, AT_DIM)

    q, k, v = heads(q), heads(k), heads(v)
    scale = AT_DIM ** -0.5
    kb = k.reshape(B, nblk, MOBA_BLOCK, AT_HEADS, AT_DIM).transpose(0, 3, 1, 2, 4)
    vb = v.reshape(B, nblk, MOBA_BLOCK, AT_HEADS, AT_DIM).transpose(0, 3, 1, 2, 4)
    k_mean = jnp.mean(kb, axis=3)
    gate = jnp.einsum('bshd,bhnd->bshn', q, k_mean)
    own = jnp.arange(s_pad) // MOBA_BLOCK
    past = jnp.arange(nblk)[None, :] < own[:, None]
    gate = jnp.where(past[None, :, None, :], gate, -jnp.inf)
    topk = min(MOBA_TOPK, nblk)
    _, sel = lax.top_k(gate, topk)
    sel_valid = sel < own[None, :, None, None]

    bias_hn = rel_bias.T.astype(f32)
    b_idx = jnp.arange(B)[:, None, None, None]
    h_idx = jnp.arange(AT_HEADS)[None, None, :, None]
    offs = jnp.arange(MOBA_BLOCK)
    n_qb = s_pad // MOBA_QBLOCK

    def qblock(j):
        start = j * MOBA_QBLOCK
        q_c = lax.dynamic_slice_in_dim(q, start, MOBA_QBLOCK, axis=1)
        sel_c = lax.dynamic_slice_in_dim(sel, start, MOBA_QBLOCK, axis=1)
        val_c = lax.dynamic_slice_in_dim(sel_valid, start, MOBA_QBLOCK, axis=1)
        q_pos = start + jnp.arange(MOBA_QBLOCK)
        own_blk = start // MOBA_BLOCK
        k_sel = kb[b_idx, h_idx, sel_c]
        v_sel = vb[b_idx, h_idx, sel_c]
        k_pos = sel_c[..., None] * MOBA_BLOCK + offs
        dist_sel = q_pos[None, :, None, None, None] - k_pos
        s_sel = (jnp.einsum('bqhd,bqhnkd->bqhnk', q_c, k_sel) * scale
                 + bias_hn[h_idx[..., None], t5_bucket(dist_sel)])
        s_sel = jnp.where(val_c[..., None], s_sel, -jnp.inf)
        k_own = lax.dynamic_index_in_dim(kb, own_blk, axis=2, keepdims=False)
        v_own = lax.dynamic_index_in_dim(vb, own_blk, axis=2, keepdims=False)
        dist_own = q_pos[:, None] - (own_blk * MOBA_BLOCK + offs)[None, :]
        bias_own = bias_hn[:, t5_bucket(dist_own)].transpose(1, 0, 2)[None]
        s_own = jnp.einsum('bqhd,bhkd->bqhk', q_c, k_own) * scale + bias_own
        s_own = jnp.where((dist_own >= 0)[None, :, None, :], s_own, -jnp.inf)
        logits = jnp.concatenate(
            [s_sel.reshape(B, MOBA_QBLOCK, AT_HEADS, topk * MOBA_BLOCK), s_own], axis=-1)
        p = jax.nn.softmax(logits, axis=-1)
        p_sel = p[..., :topk * MOBA_BLOCK].reshape(B, MOBA_QBLOCK, AT_HEADS, topk, MOBA_BLOCK)
        p_own = p[..., topk * MOBA_BLOCK:]
        return (jnp.einsum('bqhnk,bqhnkd->bqhd', p_sel, v_sel)
                + jnp.einsum('bqhk,bhkd->bqhd', p_own, v_own))

    out = lax.map(qblock, jnp.arange(n_qb))
    out = out.transpose(1, 0, 2, 3, 4).reshape(B, s_pad, AT_WIDTH)
    return out[:, :S]

def short_conv_mixer(b_gate, c_gate, h, conv_w):
    u = c_gate * h
    y = lax.conv_general_dilated(u, conv_w[:, None, :], window_strides=(1,),
                                 padding=[(CV_KERNEL - 1, 0)],
                                 dimension_numbers=('NWC', 'WIO', 'NWC'),
                                 feature_group_count=CV_WIDTH)
    return b_gate * y

def hybrid_mixer(h, w_in, w_out, lb, hg_norm_w, conv_w, rel_bias):
    z = h @ w_in
    splits = np.cumsum([HG_WIDTH] * 4 + [AT_WIDTH] * 3 + [CV_WIDTH] * 2).tolist()
    hq, hf, hi, hg, aq, ak, av, cb, cc, ch = jnp.split(z, splits, axis=-1)
    o_hg = hgrn2_mixer(hq, hf, hi, hg, lb, hg_norm_w).astype(h.dtype)
    o_at = moba_mixer(aq, ak, av, rel_bias).astype(h.dtype)
    o_cv = short_conv_mixer(cb, cc, ch, conv_w)
    o = jnp.concatenate([o_hg, o_at, o_cv], axis=-1)
    return o @ w_out

def setup_inputs(seed: int = 0) -> dict:
    key = jax.random.key(seed)
    ks = jax.random.split(key, 16)
    f32 = jnp.float32

    def nrm(k, shape, fan_in):
        return jax.random.normal(k, shape, f32) * (fan_in ** -0.5)

    return {
        'x': jax.random.normal(ks[0], (BATCH, SEQ, D_MODEL), f32),
        'norm_w': 1.0 + 0.05 * jax.random.normal(ks[1], (DEPTH, 6, D_MODEL), f32),
        'ffn1_wg': nrm(ks[2], (DEPTH, D_MODEL, D_FF), D_MODEL),
        'ffn1_wu': nrm(ks[3], (DEPTH, D_MODEL, D_FF), D_MODEL),
        'ffn1_wd': nrm(ks[4], (DEPTH, D_FF, D_MODEL), D_FF),
        'mix_w_in': nrm(ks[5], (DEPTH, D_MODEL, D_IN), D_MODEL),
        'mix_w_out': nrm(ks[6], (DEPTH, D_MIX, D_MODEL), D_MIX),
        'hg_lb': jax.random.normal(ks[7], (DEPTH, HG_WIDTH), f32),
        'hg_norm_w': 1.0 + 0.05 * jax.random.normal(ks[8], (DEPTH, HG_DIM), f32),
        'conv_w': nrm(ks[9], (DEPTH, CV_KERNEL, CV_WIDTH), CV_KERNEL),
        'ffn2_wg': nrm(ks[10], (DEPTH, D_MODEL, D_FF), D_MODEL),
        'ffn2_wu': nrm(ks[11], (DEPTH, D_MODEL, D_FF), D_MODEL),
        'ffn2_wd': nrm(ks[12], (DEPTH, D_FF, D_MODEL), D_FF),
        'rel_bias': 0.5 * jax.random.normal(ks[13], (REL_BUCKETS, AT_HEADS), f32),
    }

def reference(x, norm_w, ffn1_wg, ffn1_wu, ffn1_wd, mix_w_in, mix_w_out, hg_lb, hg_norm_w,
              conv_w, ffn2_wg, ffn2_wu, ffn2_wd, rel_bias):
    lb_soft = jax.nn.softmax(hg_lb.astype(jnp.float32), axis=0)
    lower_bounds = jnp.cumsum(lb_soft, axis=0) - lb_soft[0]
    for l in range(DEPTH):
        h = swiglu(rms_norm(x, norm_w[l, 0]), ffn1_wg[l], ffn1_wu[l], ffn1_wd[l])
        x = x + 0.5 * rms_norm(h, norm_w[l, 1])
        h = hybrid_mixer(rms_norm(x, norm_w[l, 2]), mix_w_in[l], mix_w_out[l], lower_bounds[l],
                         hg_norm_w[l], conv_w[l], rel_bias)
        x = x + rms_norm(h, norm_w[l, 3])
        h = swiglu(rms_norm(x, norm_w[l, 4]), ffn2_wg[l], ffn2_wu[l], ffn2_wd[l])
        x = x + 0.5 * rms_norm(h, norm_w[l, 5])
    return x


_drawn_inputs = setup_inputs


def setup_inputs(seed=0):
    import zlib

    import numpy as np

    out = dict(_drawn_inputs(seed))
    spreads = {}
    factors = {}
    for name, (base, spread) in spreads.items():
        noise = np.random.default_rng([zlib.crc32(name.encode()), seed]).standard_normal(out[name].shape)
        drawn = base * np.exp(spread * noise) if base else spread * noise
        out[name] = __import__('jax').numpy.asarray(drawn.astype(out[name].dtype))
    for name, factor in factors.items():
        out[name] = (out[name] * factor).astype(out[name].dtype)
    return out
```

```python
from contextlib import ExitStack
import math

import concourse.bass as bass
from concourse import mybir

LAYERS, SEQ, DM, DFF = 2, 256, 1024, 2816
P = 128
TILES = SEQ // P
KT = DM // P
HG_HEADS, AT_HEADS, AT_DIM = 4, 4, 64
HG_WIDTH, AT_WIDTH, CV_WIDTH, TAPS = HG_HEADS * P, AT_HEADS * AT_DIM, 256, 3
BUCKETS, MAX_DIST = 32, 1024
EPS = 1e-6
NORMS = 6
FT = DFF // P
RING = 6
HALF = 512
FFN_UNITS = 3 * FT
W_IN_BLOCKS = {"hq": 0, "hf": 4, "hi": 8, "hg": 12, "aq": 16, "ak": 18, "av": 20, "cb": 22, "cc": 24, "ch": 26}
PAIRS = [("hf", 0), ("hf", 2), ("hq", 0), ("hq", 2), ("aq", 0), ("ak", 0), ("av", 0), ("hi", 0), ("hi", 2),
         ("hg", 0), ("hg", 2), ("cc", 0), ("ch", 0), ("cb", 0)]
TOKEN_MAJOR = ("hi", "av")
OUT_ORDER = [4, 5, 6, 7, 0, 1, 2, 3]
NPAIR = len(PAIRS)
MIX_UNITS = 2 * NPAIR + KT
UNITS = 2 * FFN_UNITS + MIX_UNITS
FFN_BASE = [0, FFN_UNITS + MIX_UNITS]
MIX_BASE = FFN_UNITS
LEAD = 5
LEVELS = [64, 32, 16, 8, 4, 2, 1]
NLV = len(LEVELS)
FIRST_LEVEL_STEP = 3
FROM = 1
MASKED = -1e30
ACT_STEPS, DVE_STEPS = 34, 266
E_MAX = 1e30


def bucket(dist):
    dist = max(dist, 0)
    exact = BUCKETS // 2
    if dist < exact:
        return dist
    return min(BUCKETS - 1, exact + int(math.log(dist / exact) / math.log(MAX_DIST / exact) * (BUCKETS - exact)))


class Count:

    def __init__(self, semaphore, *rounds):
        self.semaphore, self.rounds, self.n, self.loops = semaphore, rounds, 0, []

    def enter(self, register):
        self.loops.append((register, self.n))

    def leave(self, times):
        each = self.rounds[len(self.loops) - 1]
        _, before = self.loops.pop()
        assert self.n - before == each, (self.n - before, each)
        self.n = before + each * times

    def done(self, instruction):
        instruction.then_inc(self.semaphore, 1)
        self.n += 1

    def wait(self, engine):
        value = self.n
        for (register, _), each in zip(self.loops, self.rounds):
            value = register * each + value
        engine.wait_ge(self.semaphore, value)


def trunk(nc, x_in, norm_w, f1_wg, f1_wu, f1_wd, w_in, w_out, hg_lb, hg_nw, conv_w,
          f2_wg, f2_wu, f2_wd, rel_bias, dist_onehot, out, bias_scratch):
    f32, f32r, u32 = mybir.dt.float32, mybir.dt.float32r, mybir.dt.uint32
    ALU, ACT, AX = mybir.AluOpType, mybir.ActivationFunctionType, mybir.AxisListType
    ffn_w = [(f1_wg, f1_wu, f1_wd), (f2_wg, f2_wu, f2_wd)]

    with ExitStack() as ctx:
        def sb(name, shape, dt=f32):
            return ctx.enter_context(nc.sbuf_tensor(name, shape, dt))

        def sem(name):
            return ctx.enter_context(nc.semaphore(name))

        raw = sb("raw", [P, RING, DM])
        wsp = sb("wsp", [P, RING, 2, DM], f32r)
        x = sb("x", [P, TILES, DM])
        nw = sb("nw", [P, 3, DM])
        xT = sb("xT", [P, 2, KT, SEQ], f32r)
        hT = sb("hT", [P, 2, 2, SEQ], f32r)
        mixT = sb("mixT", [P, 2, KT, SEQ], f32r)

        ident = sb("ident", [P, P])
        flip = sb("flip", [P, P])
        ones = sb("ones", [P, P])
        level_mask = sb("level_mask", [P, NLV, P // 2])
        keep = sb("keep", [P, HG_HEADS * TILES, P])
        bias = sb("bias", [P, AT_HEADS, 2 * P])
        relb = sb("relb", [BUCKETS, AT_HEADS])
        onehot = sb("onehot", [BUCKETS, 3 * P])
        brow = sb("brow", [AT_HEADS, 3 * P])
        lb_raw = sb("lb_raw", [P, LAYERS, HG_HEADS])
        lb_all = sb("lb_all", [P, LAYERS, 2 * HG_HEADS])
        lb_tmp = sb("lb_tmp", [P, 8, HG_HEADS])
        cw_all = sb("cw_all", [P, LAYERS, TAPS * 2])
        nw_all = sb("nw_all", [P, LAYERS])
        lb = sb("lb", [P, 2 * HG_HEADS])
        cw = sb("cw", [P, TAPS * 2])
        hnw = sb("hnw", [P, 1])
        eps_c = sb("eps_c", [P, 1])
        st = sb("st", [P, TILES, 8])
        spare = sb("spare", [P, 4])

        Q = sb("Q", [P, HG_HEADS, SEQ])
        B = sb("B", [P, HG_HEADS, SEQ])
        K = sb("K", [P, HG_HEADS, SEQ])
        D = sb("D", [P, HG_HEADS, SEQ])
        KL = sb("KL", [P, HG_HEADS, SEQ])
        QL = sb("QL", [P, HALF])
        S = sb("S", [P, HG_HEADS * TILES, P])
        S10 = sb("S10", [P, HG_HEADS, P])
        V = sb("V", [P, TILES, HG_WIDTH])
        G = sb("G", [P, HG_HEADS, SEQ])
        AQ = sb("AQ", [P, 2, SEQ])
        KZ = sb("KZ", [P, AT_HEADS, SEQ])
        AV = sb("AV", [P, TILES, AT_WIDTH])
        PA = sb("PA", [P, AT_HEADS, P])
        PB = sb("PB", [P, AT_HEADS, SEQ])
        PTA = sb("PTA", [P, AT_HEADS, P])
        PTB = sb("PTB", [P, 2, AT_HEADS, P])
        C = sb("C", [P, 2, SEQ])
        U = sb("U", [P, 2, SEQ + 2])
        Y = sb("Y", [P, 2, SEQ])
        smax = sb("smax", [P, 8])
        snmax = sb("snmax", [P, 8])
        ssum = sb("ssum", [P, 8])
        srec = sb("srec", [P, 8])
        flat = lambda t: t[:, :, :].rearrange("p h t -> p (h t)")
        xn = [flat(D), flat(KL)]
        tmp = [flat(Q), flat(B)]
        junk = flat(V)
        ff = [flat(K)[:, 0:HALF], flat(K)[:, HALF:2 * HALF]]

        Z = ctx.enter_context(nc.psum_tensor("Z", [P, 2, HALF], f32))
        ACC = ctx.enter_context(nc.psum_tensor("ACC", [P, 4, HALF], f32))
        AUX = ctx.enter_context(nc.psum_tensor("AUX", [P, 2, HALF], f32))

        raw_loaded = [sem(f"raw_loaded{i}") for i in range(RING)]
        hi_done, split_done, unit_used = sem("hi_done"), sem("split_done"), sem("unit_used")
        consts_loaded, x_loaded, onehot_loaded = sem("consts_loaded"), sem("x_loaded"), sem("onehot_loaded")
        nw_loaded = [sem(f"nw_loaded{i}") for i in range(3)]
        pool_chain, consts_ready, bias_ready = sem("pool_chain"), sem("consts_ready"), sem("bias_ready")
        brow_ps, brow_sb, scratch_written, hankel_loaded = (
            sem("brow_ps"), sem("brow_sb"), sem("scratch_written"), sem("hankel_loaded"))
        bias_ps, bias_sb, lb_shifted, lb_exp = sem("bias_ps"), sem("bias_sb"), sem("lb_shifted"), sem("lb_exp")
        rs_raw, xn_ready, xpose_done, xhi_done, xlo_done = (
            sem("rs_raw"), sem("xn_ready"), sem("xpose_done"), sem("xhi_done"), sem("xlo_done"))
        acc_ready, x_done = sem("acc_ready"), sem("x_done")
        e_ready, z_free, h_ready = sem("e_ready"), sem("z_free"), sem("h_ready")
        act_chain, dve_chain = sem("act_chain"), sem("dve_chain")
        z_evac, r2_ready, logf_ready = sem("z_evac"), sem("r2_ready"), sem("logf_ready")
        exponents, decays, level_in, level_ps, level_out = (
            sem("exponents"), sem("decays"), sem("level_in"), sem("level_ps"), sem("level_out"))
        qk_ps, logits, probs, pnorm, pT_ps, pT, at_ps = (
            sem("qk_ps"), sem("logits"), sem("probs"), sem("pnorm"), sem("pT_ps"), sem("pT"), sem("at_ps"))
        gate_e, gate_done, conv_in, mix_f, mix_hi, mix_lo = (
            sem("gate_e"), sem("gate_done"), sem("conv_in"), sem("mix_f"), sem("mix_hi"), sem("mix_lo"))
        o_ps, o_sq, ss_ps, o_rs, out_done = sem("o_ps"), sem("o_sq"), sem("ss_ps"), sem("o_rs"), sem("out_done")

        block = ctx.enter_context(nc.Block())

        @block.sync
        def _(sp):
            def load(layer, u, src, more=0, rounds=0, slots=1):
                if u < RING and rounds == 0:
                    sp.wait_ge(split_done, layer * (UNITS + u - RING + 1) + FROM)
                else:
                    if slots:
                        sp.wait_ge(split_done, layer * UNITS + more + (u - RING + slots) + FROM)
                sp.dma_start(raw[:, u % RING, :].rearrange("p (k n) -> p k n", n=src.shape[-1]), src)\
                  .then_inc(raw_loaded[u % RING], 16)

            def cols(w, layer, c):
                n = w.shape[2]
                return bass.AP(tensor=w.tensor, offset=sp.snap(layer * (w.shape[1] * n) + c),
                               ap=[[n, P], [P * n, KT], [1, P]])

            def rows(w, layer, r):
                n = w.shape[2]
                return bass.AP(tensor=w.tensor, offset=sp.snap(layer * (w.shape[1] * n) + r * n),
                               ap=[[n, P], [P * n, 1], [1, n]])

            with sp.Fori(0, LAYERS) as layer:
                def ffn(f):
                    wg, wu, wd = ffn_w[f]
                    base = FFN_BASE[f]
                    load(layer, base + 0, cols(wg, layer, 0))
                    load(layer, base + 1, cols(wu, layer, 0))
                    load(layer, base + 2, cols(wg, layer, P))
                    load(layer, base + 3, cols(wu, layer, P))
                    load(layer, base + 4, rows(wd, layer, 0))
                    with sp.Fori(0, (FT - 2) // 2) as j:
                        for i in range(2):
                            at = (base + 5 + 3 * i)
                            load(layer, at, cols(wg, layer, j * (2 * P) + (2 + i) * P), j * RING, 1)
                            load(layer, at + 1, cols(wu, layer, j * (2 * P) + (2 + i) * P), j * RING, 1)
                            load(layer, at + 2, rows(wd, layer, j * (2 * P) + (1 + i) * P), j * RING, 1)
                    load(layer, base + FFN_UNITS - 1, rows(wd, layer, DFF - P))

                ffn(0)
                starts = [(W_IN_BLOCKS[name] + first + c) * P for name, first in PAIRS for c in range(2)]
                starts += [kt * P for kt in OUT_ORDER] + [None]
                for i, start in enumerate(starts[:-1]):
                    load(layer, MIX_BASE + i, cols(w_in, layer, start) if i < 2 * NPAIR else rows(w_out, layer, start),
                         slots=0 if start == 0 else 2 if starts[i + 1] == 0 else 1)
                ffn(1)
            for t in range(TILES):
                sp.wait_ge(x_done, LAYERS * NORMS - TILES + t + 1 + FROM)
                sp.dma_start(out[0, t * P:(t + 1) * P, :], x[:, t, :]).then_inc(out_done, 16)
            sp.wait_ge(out_done, 16 * TILES)

        @block.gpsimd
        def _(pool):
            chained = [0]

            def link(ins):
                ins.then_inc(pool_chain, 1)
                chained[0] += 1
                pool.wait_ge(pool_chain, chained[0])

            def norm_load(i, layer):
                row = norm_w[bass.ds(layer, 1), i:i + 1, :].rearrange("a b n -> (a b) n")
                pool.dma_start(nw[:, i % 3, :], row.broadcast_to([P, DM])).then_inc(nw_loaded[i % 3], 16)

            link(pool.memset(ident[:, :], 0.0))
            link(pool.affine_select(out=ident[:, :], in_=ident[:, :], compare_op=ALU.not_equal, fill=1.0,
                                    base=0, pattern=[[-1, P]], channel_multiplier=1))
            pool.memset(eps_c[:, :], EPS).then_inc(consts_ready, 1)
            link(pool.memset(flip[:, :], 0.0))
            link(pool.affine_select(out=flip[:, :], in_=flip[:, :], compare_op=ALU.not_equal, fill=1.0,
                                    base=1 - P, pattern=[[1, P]], channel_multiplier=1))
            link(pool.memset(ones[:, :], 1.0))
            link(pool.memset(level_mask[:, :, :], 1.0))
            for n, m in enumerate(LEVELS):
                part = level_mask[:, n, :].rearrange("p (j m) -> p j m", m=m)
                link(pool.affine_select(out=part, in_=part, compare_op=ALU.is_ge, fill=0.0, base=0,
                                        pattern=[[-2 * m, P // (2 * m)], [0, m]], channel_multiplier=1))
                link(pool.affine_select(out=part, in_=part, compare_op=ALU.is_ge, fill=0.0, base=m - 1,
                                        pattern=[[2 * m, P // (2 * m)], [0, m]], channel_multiplier=-1))
            link(pool.memset(keep[:, :, :], 1.0))
            link(pool.memset(keep[:, :, 0:1], 0.0))
            link(pool.memset(KZ[:, :, :], 0.0))
            link(pool.memset(KL[:, :, :], 0.0))
            pool.memset(U[:, :, :], 0.0).then_inc(consts_ready, 1)
            pool.wait_ge(brow_sb, 1)
            pool.dma_start(bias_scratch, brow[:, :]).then_inc(scratch_written, 16)
            pool.wait_ge(scratch_written, 16)
            hankel = bass.AP(tensor=bias_scratch.tensor, offset=0, ap=[[1, P], [3 * P, AT_HEADS], [1, 2 * P]])
            pool.dma_start(S[:, :, :].rearrange("p (h a) b -> p h (a b)", a=2), hankel).then_inc(hankel_loaded, 16)
            pool.wait_ge(bias_sb, 1)
            pool.affine_select(out=bias[:, :, :], in_=bias[:, :, :], compare_op=ALU.is_ge, fill=MASKED, base=P,
                               pattern=[[0, AT_HEADS], [-1, 2 * P]], channel_multiplier=1).then_inc(bias_ready, 1)
            with pool.Fori(0, LAYERS) as layer:
                for i in range(NORMS):
                    j = i - 3
                    back = layer * NORMS + 2 * (j // 2) + 2 if j >= 0 else layer * (NORMS + 2 * (j // 2) + 2)
                    pool.wait_ge(x_done if j % 2 else xn_ready, back + FROM)
                    norm_load(i, layer)
            for i in range(3):
                pool.wait_ge(nw_loaded[i], 16 * 2 * LAYERS)

        @block.scalar
        def _(act):
            chain = Count(act_chain, ACT_STEPS)

            act.dma_start(lb_raw[:, :, :], hg_lb.rearrange("l (h p) -> p l h", p=P),
                          allow_slow_non_contiguous=True).then_inc(consts_loaded, 16)
            act.dma_start(cw_all[:, :, :].rearrange("p l (w c) -> p (l w) c", c=2),
                          conv_w.rearrange("l w (c p) -> p (l w) c", p=P), allow_slow_non_contiguous=True).then_inc(consts_loaded, 16)
            act.dma_start(nw_all[:, :], hg_nw.rearrange("l p -> p l"), allow_slow_non_contiguous=True).then_inc(consts_loaded, 16)
            act.dma_start(relb[:, :], rel_bias).then_inc(onehot_loaded, 16)
            act.dma_start(onehot[:, :], dist_onehot).then_inc(onehot_loaded, 16)
            act.dma_start(x[:, :, :], x_in[0].rearrange("(t p) n -> p t n", p=P)).then_inc(x_loaded, 16)

            act.wait_ge(lb_shifted, 1)
            act.activation(lb_tmp[:, 1:3, :], lb_tmp[:, 1:3, :], ACT.Exp).then_inc(lb_exp, 1)
            act.wait_ge(x_loaded, 16)
            act.wait_ge(consts_ready, 1)

            with act.Fori(0, LAYERS) as layer:
                chain.enter(layer)

                def U_(u, more=0):
                    return layer * UNITS + more + u

                def split(u, more=0, rounds=0):
                    act.wait_ge(raw_loaded[u % RING], (layer * (UNITS // RING) + rounds + (u // RING + 1)) * 16)
                    act.wait_ge(unit_used, (layer * UNITS if u < RING else U_(u - RING + 1, more)) + FROM)
                    act.activation(wsp[:, u % RING, 0, :], raw[:, u % RING, :], ACT.Copy).then_inc(hi_done, 1)

                def inverse_rms(src, t, n):
                    chain.done(act.activation(junk, src, ACT.Square, accum_out=st[:, t, 0:1]))
                    chain.wait(act)
                    chain.done(act.activation(st[:, t, 1:2], st[:, t, 0:1], ACT.Ln, bias=eps_c[:, :], scale=1.0 / DM))
                    chain.wait(act)
                    act.activation(st[:, t, 2:3], st[:, t, 1:2], ACT.Exp, scale=-0.5).then_inc(rs_raw, 1)

                def pre(s):
                    for t in range(TILES):
                        act.wait_ge(x_done, layer * NORMS + 2 * s + (0 if s == 0 else t - 1) + FROM)
                        inverse_rms(x[:, t, :], t, s)
                    for t in range(TILES):
                        for h in range(2):
                            act.wait_ge(xpose_done, layer * 12 + 4 * s + 2 * t + h + 1)
                            act.activation(xT[:, 0, 4 * h:4 * h + 4, t * P:(t + 1) * P],
                                           AUX[:, h, :].rearrange("p (k n) -> p k n", k=4), ACT.Copy)\
                               .then_inc(xhi_done, 1)

                def post(s):
                    for t in range(TILES):
                        if t == 0:
                            act.wait_ge(acc_ready, layer * 3 + s + 1)
                        else:
                            act.wait_ge(unit_used, U_((FFN_UNITS, FFN_BASE[1], UNITS)[s]) + FROM)
                        inverse_rms(ACC[:, 2 * t:2 * t + 2, :].rearrange("p a b -> p (a b)"), t, s)

                def ffn(f):
                    base = FFN_BASE[f]

                    def gate(g, more=0):
                        used = 3 * g if g else 1
                        act.wait_ge(unit_used, U_(base + used + 1, more) + FROM)
                        act.activation(ff[g % 2][:, 0:SEQ], Z[:, g % 2, 0:SEQ], ACT.Exp, scale=-1.0)\
                           .then_inc(e_ready, 1)

                    for g in range(2):
                        gate(g)
                        for i in range(3):
                            split(base + LEAD + 3 * g + i)
                    with act.Fori(0, (FT - 4) // 2) as j:
                        for g in range(2, 4):
                            gate(g, j * RING)
                            for i in range(3):
                                split(base + LEAD + 3 * g + i, j * RING, j)
                    last = FT - 2
                    gate(last)
                    split(base + FFN_UNITS - 1)
                    if f == 0:
                        split(base + FFN_UNITS)
                    gate(last + 1)
                    if f == 0:
                        for i in range(1, LEAD):
                            split(base + FFN_UNITS + i)

                def mixer():
                    base = MIX_BASE

                    def evac(p, dst, src):
                        act.activation(dst, src, ACT.Copy).then_inc(z_evac, 1)

                    for q in range(NPAIR + KT // 2):
                        if q < NPAIR:
                            act.wait_ge(unit_used, U_(base + 2 * q + 2) + FROM)
                            z = Z[:, q % 2, :]
                            name, first = PAIRS[q]
                            two = z.rearrange("p (h t) -> p h t", h=2)
                            if name == "hf":
                                act.activation(K[:, first:first + 2, :], two, ACT.Exp, scale=-1.0).then_inc(z_evac, 1)
                            elif name == "hq":
                                evac(q, Q[:, first:first + 2, :], two)
                            elif name == "aq":
                                evac(q, AQ[:, :, :], two)
                            elif name == "ak":
                                chain.done(act.activation(KZ[0:AT_DIM, 0:4:2, :], two[0:AT_DIM, :, :], ACT.Copy))
                                evac(q, KZ[AT_DIM:P, 1:4:2, :], two[AT_DIM:P, :, :])
                            elif name == "av":
                                evac(q, AV[:, :, :], two)
                            elif name == "hi":
                                evac(q, V[:, :, first * P:(first + 2) * P], two)
                            elif name == "hg":
                                act.activation(G[:, first:first + 2, :], two, ACT.Exp, scale=-1.0).then_inc(gate_e, 1)
                            elif name == "cc":
                                evac(q, C[:, :, :], two)
                        if q == 1:
                            act.wait_ge(r2_ready, layer + 1)
                            for h in range(HG_HEADS):
                                act.activation(B[:, h, :], D[:, h, :], ACT.Ln, bias=lb[:, h:h + 1])\
                                   .then_inc(logf_ready, 1)
                        n = q - FIRST_LEVEL_STEP
                        if 0 <= n <= NLV:
                            act.wait_ge(exponents, layer * (NLV + 1) + n + 1)
                            if n < NLV:
                                v = flat(D).rearrange("p (g q m) -> p g q m", q=2, m=LEVELS[n])
                                chain.done(act.activation(v[:, :, 0, :], v[:, :, 0, :], ACT.Exp, scale=-1.0))
                                act.activation(v[:, :, 1, :], v[:, :, 1, :], ACT.Exp).then_inc(decays, 1)
                            else:
                                chain.done(act.activation(D[:, :, 0:P], D[:, :, 0:P], ACT.Exp, scale=-1.0))
                                act.activation(D[:, :, P:SEQ], B[:, :, P:SEQ], ACT.Exp).then_inc(decays, 1)
                        if q == 7:
                            act.wait_ge(logits, layer + 1)
                            for h in range(AT_HEADS):
                                act.activation(PA[:, h, :], PA[:, h, :], ACT.Exp, bias=snmax[:, h:h + 1],
                                               accum_out=ssum[:, h:h + 1]).then_inc(probs, 1)
                                act.activation(PB[:, h, :], PB[:, h, :], ACT.Exp, bias=snmax[:, 4 + h:5 + h],
                                               accum_out=ssum[:, 4 + h:5 + h]).then_inc(probs, 1)
                        if q == 10:
                            act.wait_ge(pT_ps, layer + 1)
                            act.activation(PTA[:, :, :], AUX[:, 0, :].rearrange("p (h t) -> p h t", h=4), ACT.Copy)\
                               .then_inc(pT, 1)
                            act.activation(PTB[:, :, :, :].rearrange("p a h t -> p a (h t)"), ACC[:, 2:4, :], ACT.Copy)\
                               .then_inc(pT, 1)
                        if q == 12:
                            act.wait_ge(at_ps, layer + 1)
                            act.activation(mixT[:, 0, 4:6, :], AUX[:, 1, :].rearrange("p (a t) -> p a t", a=2),
                                           ACT.Copy).then_inc(mix_hi, 1)
                        for i in range(2):
                            split(base + LEAD + 2 * q + i)
                        if q == NPAIR - 1:
                            act.wait_ge(mix_f, layer * 2 + 1)
                            act.activation(mixT[:, 0, 6:8, :], Y[:, :, :], ACT.Copy).then_inc(mix_hi, 1)
                            act.wait_ge(o_ps, layer + 1)
                            act.activation(flat(D), AUX[:, :, :].rearrange("p a b -> p (a b)"), ACT.Square)\
                               .then_inc(o_sq, 1)
                        if q == NPAIR:
                            act.wait_ge(ss_ps, layer + 1)
                            chain.done(act.activation(flat(K), Z[:, :, :].rearrange("p a b -> p (a b)"), ACT.Ln,
                                                      bias=eps_c[:, :], scale=1.0 / P))
                            chain.wait(act)
                            act.activation(flat(K), flat(K), ACT.Exp, scale=-0.5).then_inc(o_rs, 1)
                        if q == NPAIR + 1:
                            act.wait_ge(mix_f, layer * 2 + 2)
                            act.activation(mixT[:, 0, 0:4, :], Q[:, :, :], ACT.Copy).then_inc(mix_hi, 1)

                for u in range(LEAD):
                    split(u)
                pre(0)
                ffn(0)
                post(0)
                pre(1)
                mixer()
                post(1)
                pre(2)
                ffn(1)
                post(2)
                chain.leave(LAYERS)

        @block.vector
        def _(dve):
            chain = Count(dve_chain, DVE_STEPS, 8)

            def link(ins):
                chain.done(ins)
                chain.wait(dve)

            for i, started in enumerate((split_done, xn_ready, x_done)):
                dve.memset(spare[:, i:i + 1], 0.0).then_inc(started, FROM)
            dve.wait_ge(brow_ps, 1)
            dve.tensor_copy(brow[:, :], AUX[0:AT_HEADS, 0, 0:3 * P]).then_inc(brow_sb, 1)
            dve.wait_ge(consts_loaded, 48)
            a = [lb_raw[:, l, :] for l in range(LAYERS)]
            mx, e0, e1, tot, rec, s0, s1, cum = [lb_tmp[:, i, :] for i in range(8)]
            link(dve.tensor_tensor(mx, a[0], a[1], ALU.max))
            link(dve.tensor_tensor(e0, a[0], mx, ALU.subtract))
            dve.tensor_tensor(e1, a[1], mx, ALU.subtract).then_inc(lb_shifted, 1)
            dve.wait_ge(lb_exp, 1)
            link(dve.tensor_tensor(tot, e0, e1, ALU.add))
            link(dve.reciprocal(rec, tot))
            link(dve.tensor_tensor(s0, e0, rec, ALU.mult))
            link(dve.tensor_tensor(s1, e1, rec, ALU.mult))
            link(dve.tensor_tensor(cum, s0, s1, ALU.add))
            link(dve.tensor_tensor(lb_all[:, 0, 0:HG_HEADS], s0, s0, ALU.subtract))
            link(dve.tensor_tensor(lb_all[:, 1, 0:HG_HEADS], cum, s0, ALU.subtract))
            link(dve.tensor_scalar(lb_all[:, :, HG_HEADS:], lb_all[:, :, 0:HG_HEADS], -1.0, 1.0, ALU.mult, ALU.add))

            dve.wait_ge(bias_ps, 1)
            dve.tensor_copy(bias[:, :, :].rearrange("p (a h) u -> p a (h u)", a=2), ACC[:, 0:2, :]).then_inc(bias_sb, 1)
            dve.wait_ge(consts_ready, 2)

            with dve.Fori(0, LAYERS) as layer:
                chain.enter(layer)

                def U_(u, more=0):
                    return layer * UNITS + more + u

                def split(u, more=0):
                    dve.wait_ge(hi_done, U_(u + 1, more))
                    dve.tensor_tensor(wsp[:, u % RING, 1, :], raw[:, u % RING, :],
                                      wsp[:, u % RING, 0, :].bitcast(f32), ALU.subtract).then_inc(split_done, 1)

                def refine(t, n, factor):
                    dve.wait_ge(rs_raw, layer * 12 + n + 1)
                    v, y = st[:, t, 3:4], st[:, t, 2:3]
                    link(dve.tensor_scalar(v, st[:, t, 0:1], 1.0 / DM, EPS, ALU.mult, ALU.add))
                    link(dve.scalar_tensor_tensor(st[:, t, 4:5], v, y, y, ALU.mult, ALU.mult))
                    link(dve.tensor_scalar(st[:, t, 5:6], st[:, t, 4:5], -0.5 * factor, 1.5 * factor, ALU.mult, ALU.add))
                    link(dve.tensor_tensor(st[:, t, 6:7], st[:, t, 5:6], y, ALU.mult))
                    return st[:, t, 6:7]

                def weights_of(i):
                    dve.wait_ge(nw_loaded[i % 3], (layer * 2 + (i // 3 + 1)) * 16)
                    return nw[:, i % 3, :]

                def pre(s):
                    w = weights_of(2 * s)
                    for t in range(TILES):
                        r = refine(t, 4 * s + t, 1.0)
                        dve.scalar_tensor_tensor(xn[t], x[:, t, :], r, w, ALU.mult, ALU.mult).then_inc(xn_ready, 1)
                    for t in range(TILES):
                        for h in range(2):
                            dve.wait_ge(xhi_done, layer * 12 + 4 * s + 2 * t + h + 1)
                            at = slice(t * P, (t + 1) * P)
                            dve.tensor_tensor(xT[:, 1, 4 * h:4 * h + 4, at],
                                              AUX[:, h, :].rearrange("p (k n) -> p k n", k=4),
                                              xT[:, 0, 4 * h:4 * h + 4, at].bitcast(f32), ALU.subtract)\
                               .then_inc(xlo_done, 1)

                def post(s, factor):
                    w = weights_of(2 * s + 1)
                    for t in range(TILES):
                        r = refine(t, 4 * s + 2 + t, factor)
                        link(dve.scalar_tensor_tensor(tmp[t], ACC[:, 2 * t:2 * t + 2, :].rearrange("p a b -> p (a b)"),
                                                      r, w, ALU.mult, ALU.mult))
                        dve.tensor_tensor(x[:, t, :], x[:, t, :], tmp[t], ALU.add).then_inc(x_done, 1)

                def ffn(f):
                    base = FFN_BASE[f]

                    def hidden(g, more=0, rounds=0):
                        dve.wait_ge(e_ready, layer * (2 * FT) + rounds + (FT * f + g + 1))
                        e, h = ff[g % 2][:, 0:SEQ], ff[g % 2][:, SEQ:2 * SEQ]
                        link(dve.tensor_scalar(e, e, 1.0, None, ALU.add))
                        link(dve.reciprocal(e, e))
                        link(dve.tensor_tensor(e, Z[:, g % 2, 0:SEQ], e, ALU.mult))
                        chain.done(dve.tensor_tensor(h, Z[:, g % 2, SEQ:2 * SEQ], e, ALU.mult))
                        chain.wait(dve)
                        if g >= 2:
                            dve.wait_ge(unit_used, U_(base + 4 + 3 * (g - 2) + 1, more) + FROM)
                        dve.tensor_copy(hT[:, g % 2, 0, :], h).then_inc(z_free, 1)
                        dve.wait_ge(z_free, layer * (2 * FT) + rounds + (FT * f + g + 1))
                        dve.tensor_tensor(hT[:, g % 2, 1, :], h, hT[:, g % 2, 0, :].bitcast(f32), ALU.subtract)\
                           .then_inc(h_ready, 1)

                    for g in range(2):
                        hidden(g)
                        for i in range(3):
                            split(base + LEAD + 3 * g + i)
                    with dve.Fori(0, (FT - 4) // 2) as j:
                        chain.enter(j)
                        for g in range(2, 4):
                            hidden(g, j * RING, j * 2)
                            for i in range(3):
                                split(base + LEAD + 3 * g + i, j * RING)
                        chain.leave((FT - 4) // 2)
                    last = FT - 2
                    hidden(last)
                    split(base + FFN_UNITS - 1)
                    if f == 0:
                        split(base + FFN_UNITS)
                    hidden(last + 1)
                    if f == 0:
                        for i in range(1, LEAD):
                            split(base + FFN_UNITS + i)

                def mixer():
                    base = MIX_BASE
                    z_of = lambda q: Z[:, q % 2, :].rearrange("p (h t) -> p h t", h=2)
                    link(dve.memset(S[:, :, :], 0.0))
                    for q in range(NPAIR + KT // 2):
                        if q == 1:
                            dve.wait_ge(z_evac, layer * 10 + 2)
                            link(dve.tensor_scalar(flat(D), flat(K), E_MAX, 1.0, ALU.min, ALU.add))
                            link(dve.reciprocal(flat(B), flat(D)))
                            for h in range(HG_HEADS):
                                ins = dve.tensor_scalar(D[:, h, :], B[:, h, :], lb[:, HG_HEADS + h:HG_HEADS + h + 1],
                                                        None, ALU.mult)
                                if h < HG_HEADS - 1:
                                    chain.done(ins)
                            ins.then_inc(r2_ready, 1)
                            dve.wait_ge(r2_ready, layer + 1)
                            link(dve.scalar_tensor_tensor(flat(K), flat(K), E_MAX, flat(D), ALU.min, ALU.mult))
                        if q == 2:
                            dve.wait_ge(logf_ready, layer * HG_HEADS + HG_HEADS)
                            link(dve.tensor_tensor_scan(flat(B), keep[:, :, :].rearrange("p g t -> p (g t)"), flat(B),
                                                        0.0, ALU.mult, ALU.add))
                        n = q - FIRST_LEVEL_STEP
                        if 1 <= n <= NLV:
                            dve.wait_ge(level_in, layer * (NLV + 1) + n)
                        if 0 <= n < NLV:
                            m = LEVELS[n]
                            v = flat(B).rearrange("p (g n) -> p g n", n=2 * m)
                            o = flat(D).rearrange("p (g n) -> p g n", n=2 * m)
                            dve.tensor_tensor(o, v, v[:, :, m - 1:m].broadcast_to([P, 512 // m, 2 * m]),
                                              ALU.subtract).then_inc(exponents, 1)
                        if n == NLV:
                            dve.tensor_tensor(D[:, :, 0:P], B[:, :, 0:P],
                                              B[:, :, P - 1:P].broadcast_to([P, HG_HEADS, P]), ALU.subtract)\
                               .then_inc(exponents, 1)
                        for i in range(2):
                            split(base + LEAD + 2 * q + i)
                        if 0 <= n <= NLV:
                            dve.wait_ge(decays, layer * (NLV + 1) + n + 1)
                            dve.wait_ge(z_evac, layer * 10 + 4)
                            if n:
                                dve.wait_ge(level_ps, layer * (NLV + 2) + n)
                            if n < NLV:
                                by = lambda t: flat(t).rearrange("p (g q m) -> p g q m", q=2, m=LEVELS[n])
                                chain.done(dve.tensor_tensor(by(KL)[:, :, 0, :], by(K)[:, :, 0, :], by(D)[:, :, 0, :],
                                                             ALU.mult))
                                dve.tensor_tensor(QL[:, :].rearrange("p (g m) -> p g m", m=LEVELS[n]),
                                                  by(Q)[:, :, 1, :], by(D)[:, :, 1, :], ALU.mult).then_inc(level_in, 1)
                            else:
                                chain.done(dve.tensor_tensor(KL[:, :, 0:P], K[:, :, 0:P], D[:, :, 0:P], ALU.mult))
                                dve.tensor_tensor(QL[:, :].rearrange("p (g m) -> p g m", m=P),
                                                  Q[:, :, P:SEQ], D[:, :, P:SEQ], ALU.mult).then_inc(level_in, 1)
                        c = n - 1
                        if 0 <= c <= NLV + 1:
                            dve.wait_ge(level_ps, layer * (NLV + 2) + c + 1)
                            if c:
                                dve.wait_ge(level_out, layer * (NLV + 2) + c)
                            if c < NLV:
                                m = LEVELS[c]
                                into = S[:, :, :].rearrange("p g (j q m) -> p g j q m", q=2, m=m)[:, :, :, 1, :]
                                mask = level_mask[:, c, :].bitcast(u32).rearrange("p (g j m) -> p g j m", g=1, m=m)\
                                    .broadcast_to([P, 8, P // (2 * m), m])
                                dve.memset(spare[:, 3:4], 0.0)
                                dve.copy_predicated(into, mask, ACC[:, c % 2, :].rearrange(
                                    "p (g j m) -> p g j m", g=8, m=m)).then_inc(level_out, 1)
                            elif c == NLV:
                                dve.tensor_copy(S10[:, :, :], ACC[:, NLV % 2, :].rearrange("p (h t) -> p h t", h=4))\
                                   .then_inc(level_out, 1)
                            else:
                                mask = ident[:, :].bitcast(u32).rearrange("p (g t) -> p g t", g=1).broadcast_to([P, 8, P])
                                dve.memset(spare[:, 3:4], 0.0)
                                dve.copy_predicated(S[:, :, :], mask, ACC[:, 0:2, :].rearrange(
                                    "p a (g t) -> p (a g) t", t=P)).then_inc(level_out, 1)
                        if q == 6:
                            dve.wait_ge(bias_ready, 1)
                            dve.wait_ge(qk_ps, layer + 1)
                            scale = float(AT_DIM) ** -0.5
                            chain.done(dve.scalar_tensor_tensor(
                                PA[:, :, :], AUX[:, 0, :].rearrange("p (h t) -> p h t", h=4), scale,
                                bias[:, :, P:2 * P], ALU.mult, ALU.add))
                            link(dve.scalar_tensor_tensor(
                                PB[:, :, :], ACC[:, 2:4, :].rearrange("p a (h t) -> p (a h) t", t=SEQ), scale,
                                bias[:, :, :], ALU.mult, ALU.add))
                            chain.done(dve.reduce_max(smax[:, 0:4], PA[:, :, :], AX.X))
                            link(dve.reduce_max(smax[:, 4:8], PB[:, :, :], AX.X))
                            dve.tensor_scalar(snmax[:, :], smax[:, :], -1.0, None, ALU.mult).then_inc(logits, 1)
                        if q == 8:
                            dve.wait_ge(probs, layer * 8 + 8)
                            link(dve.reciprocal(srec[:, :], ssum[:, :]))
                            chain.done(dve.tensor_tensor(PA[:, :, :], PA[:, :, :], srec[:, 0:4].rearrange(
                                "p (h a) -> p h a", a=1).broadcast_to([P, 4, P]), ALU.mult))
                            dve.tensor_tensor(PB[:, :, :], PB[:, :, :], srec[:, 4:8].rearrange(
                                "p (h a) -> p h a", a=1).broadcast_to([P, 4, SEQ]), ALU.mult).then_inc(pnorm, 1)
                        if q < NPAIR and PAIRS[q][0] == "hg":
                            i = PAIRS[q][1]
                            dve.wait_ge(gate_e, layer * 2 + i // 2 + 1)
                            part = G[:, i:i + 2, :]
                            link(dve.tensor_scalar(part, part, 1.0, None, ALU.add))
                            link(dve.reciprocal(part, part))
                            dve.tensor_tensor(part, z_of(q), part, ALU.mult).then_inc(gate_done, 1)
                        if q == 12:
                            dve.wait_ge(mix_hi, layer * 3 + 1)
                            dve.tensor_tensor(mixT[:, 1, 4:6, :], AUX[:, 1, :].rearrange("p (a t) -> p a t", a=2),
                                              mixT[:, 0, 4:6, :].bitcast(f32), ALU.subtract).then_inc(mix_lo, 1)
                            dve.wait_ge(z_evac, layer * 10 + 10)
                            dve.wait_ge(unit_used, U_(base + 2 * q + 2) + FROM)
                            dve.tensor_tensor(U[:, :, 2:], z_of(q), C[:, :, :], ALU.mult).then_inc(conv_in, 1)
                            dve.wait_ge(conv_in, layer + 1)
                            tap = lambda i, c_: cw[:, 2 * i + c_:2 * i + c_ + 1]
                            for c_ in range(2):
                                chain.done(dve.tensor_scalar(Y[:, c_, :], U[:, c_, 2:], tap(2, c_), None, ALU.mult))
                            for i in (1, 0):
                                chain.wait(dve)
                                for c_ in range(2):
                                    chain.done(dve.scalar_tensor_tensor(Y[:, c_, :], U[:, c_, i:i + SEQ], tap(i, c_),
                                                                        Y[:, c_, :], ALU.mult, ALU.add))
                            chain.wait(dve)
                        if q == NPAIR - 1:
                            dve.wait_ge(unit_used, U_(base + 2 * q + 2) + FROM)
                            dve.tensor_tensor(Y[:, :, :], z_of(q), Y[:, :, :], ALU.mult).then_inc(mix_f, 1)
                            dve.wait_ge(mix_hi, layer * 3 + 2)
                            dve.tensor_tensor(mixT[:, 1, 6:8, :], Y[:, :, :], mixT[:, 0, 6:8, :].bitcast(f32),
                                              ALU.subtract).then_inc(mix_lo, 1)
                            dve.wait_ge(gate_done, layer * 2 + 2)
                            dve.wait_ge(o_sq, layer + 1)
                            link(dve.scalar_tensor_tensor(flat(Q), AUX[:, :, :].rearrange("p a b -> p (a b)"),
                                                          hnw[:, :], flat(G), ALU.mult, ALU.mult))
                        if q == NPAIR + 1 - 1:
                            dve.wait_ge(o_rs, layer + 1)
                            dve.tensor_tensor(flat(Q), flat(Q), flat(K), ALU.mult).then_inc(mix_f, 1)
                        if q == NPAIR + 1:
                            dve.wait_ge(mix_hi, layer * 3 + 3)
                            dve.tensor_tensor(mixT[:, 1, 0:4, :], Q[:, :, :], mixT[:, 0, 0:4, :].bitcast(f32),
                                              ALU.subtract).then_inc(mix_lo, 1)

                chain.done(dve.tensor_copy(lb[:, :], lb_all[:, bass.ds(layer, 1), :].rearrange("p a n -> p (a n)")))
                chain.done(dve.tensor_copy(cw[:, :], cw_all[:, bass.ds(layer, 1), :].rearrange("p a n -> p (a n)")))
                link(dve.tensor_copy(hnw[:, :], nw_all[:, bass.ds(layer, 1)]))
                for u in range(LEAD):
                    split(u)
                pre(0)
                ffn(0)
                post(0, 0.5)
                pre(1)
                mixer()
                post(1, 1.0)
                pre(2)
                ffn(1)
                post(2, 0.5)
                chain.leave(LAYERS)

        @block.tensor
        def _(pe):
            pe.wait_ge(onehot_loaded, 32)
            pe.matmul(AUX[0:AT_HEADS, 0, 0:3 * P], relb[:, :], onehot[:, :], start=True, stop=True).then_inc(brow_ps, 1)
            pe.wait_ge(hankel_loaded, 16)
            pe.wait_ge(consts_ready, 2)
            for a in range(2):
                if a:
                    ins.then_inc(unit_used, FROM)
                ins = pe.matmul(ACC[:, a, :], flip[:, :], S[:, 4 * a:4 * a + 4, :].rearrange("p g t -> p (g t)"),
                                start=True, stop=True)
            ins.then_inc(bias_ps, 1)

            PRODUCTS = ((0, 0), (0, 1), (1, 0))

            with pe.Fori(0, LAYERS) as layer:
                def U_(u, more=0):
                    return layer * UNITS + more + u

                def feature_major(dst, u, more=0):
                    pe.wait_ge(split_done, U_(u + 1, more) + FROM)
                    for k in range(KT):
                        for a, b in PRODUCTS:
                            ins = pe.matmul(dst, wsp[:, u % RING, a, k * P:(k + 1) * P], xT[:, b, k, :],
                                            start=(k == 0 and a + b == 0), stop=(k == KT - 1 and a == 1))
                    ins.then_inc(unit_used, 1)

                def token_major(dst, u):
                    pe.wait_ge(split_done, U_(u + 2) + FROM)
                    s = u % RING
                    for t in range(TILES):
                        for k in range(KT):
                            for a, b in PRODUCTS:
                                ins = pe.matmul(dst[:, t * SEQ:(t + 1) * SEQ].rearrange("p (c n) -> p c n", c=2),
                                                xT[:, b, k, t * P:(t + 1) * P],
                                                wsp[:, s:s + 2, a, k * P:(k + 1) * P],
                                                start=(k == 0 and a + b == 0), stop=(k == KT - 1 and a == 1))
                    ins.then_inc(unit_used, 2)

                def down(left, u, first, last, more=0):
                    pe.wait_ge(split_done, U_(u + 1, more) + FROM)
                    for t in range(TILES):
                        for a, b in PRODUCTS:
                            for h in range(2):
                                ins = pe.matmul(ACC[:, 2 * t + h, :], left[:, b, t * P:(t + 1) * P],
                                                wsp[:, u % RING, a, h * HALF:(h + 1) * HALF],
                                                start=(first and a + b == 0), stop=(last and a == 1))
                        if last and t == 0:
                            ins.then_inc(acc_ready, 1)
                    ins.then_inc(unit_used, 1)

                def pre(s):
                    for t in range(TILES):
                        pe.wait_ge(xn_ready, layer * NORMS + 2 * s + t + 1 + FROM)
                        for h in range(2):
                            if t:
                                pe.wait_ge(xlo_done, layer * 12 + 4 * s + h + 1)
                            for k in range(4):
                                ins = pe.transpose(AUX[:, h, k * P:(k + 1) * P],
                                                   xn[t][:, (4 * h + k) * P:(4 * h + k + 1) * P], ident[:, :])
                            ins.then_inc(xpose_done, 1)
                    pe.wait_ge(xlo_done, layer * 12 + 4 * s + 4)

                def ffn(f):
                    base = FFN_BASE[f]

                    def gate_up(g, more=0, rounds=0):
                        u = base + (3 * g - 1 if g else 0)
                        if g >= 2:
                            pe.wait_ge(z_free, layer * (2 * FT) + rounds + (FT * f + g - 1))
                        feature_major(Z[:, g % 2, 0:SEQ], u, more)
                        feature_major(Z[:, g % 2, SEQ:2 * SEQ], u + 1, more)

                    def down_of(g, more=0, rounds=0, first=False, last=False):
                        pe.wait_ge(h_ready, layer * (2 * FT) + rounds + (FT * f + g + 1))
                        down(hT[:, g % 2], base + (4 + 3 * g if g < FT - 1 else FFN_UNITS - 1), first, last, more)

                    gate_up(0)
                    gate_up(1)
                    down_of(0, first=True)
                    with pe.Fori(0, (FT - 2) // 2) as j:
                        for g in range(2, 4):
                            gate_up(g, j * RING, j * 2)
                            down_of(g - 1, j * RING, j * 2)
                    down_of(FT - 1, last=True)

                def mixer():
                    base = MIX_BASE
                    for q in range(NPAIR):
                        if q == 11:
                            pe.wait_ge(gate_done, layer * 2 + 1)
                        elif q == 12:
                            pe.wait_ge(gate_done, layer * 2 + 2)
                        elif q >= 2:
                            pe.wait_ge(z_evac, layer * 10 + min(q - 1, 10))
                        name, _ = PAIRS[q]
                        if name in TOKEN_MAJOR:
                            token_major(Z[:, q % 2, :], base + 2 * q)
                        else:
                            feature_major(Z[:, q % 2, 0:SEQ], base + 2 * q)
                            feature_major(Z[:, q % 2, SEQ:2 * SEQ], base + 2 * q + 1)
                        n = q - FIRST_LEVEL_STEP - 1
                        if 0 <= n <= NLV:
                            pe.wait_ge(level_in, layer * (NLV + 1) + n + 1)
                            if n >= 2:
                                pe.wait_ge(level_out, layer * (NLV + 2) + n - 1)
                            w = P // 2 if n < NLV else P
                            for i in range(HALF // w):
                                key = flat(KL)[:, i * P:(i + 1) * P] if n < NLV else KL[:, i, 0:P]
                                ins = pe.matmul(ACC[:, n % 2, i * w:(i + 1) * w], key, QL[:, i * w:(i + 1) * w],
                                                start=True, stop=True)
                            ins.then_inc(level_ps, 1)
                        if n == NLV + 1:
                            pe.wait_ge(level_out, layer * (NLV + 2) + n)
                            for i in range(8):
                                ins = pe.matmul(ACC[:, i // 4, i % 4 * P:(i % 4 + 1) * P], flat(K)[:, i * P:(i + 1) * P],
                                                flat(Q)[:, i * P:(i + 1) * P], start=True, stop=True)
                            ins.then_inc(level_ps, 1)
                        if q == 6:
                            pe.wait_ge(z_evac, layer * 10 + 6)
                            for h in range(AT_HEADS):
                                pe.matmul(AUX[:, 0, h * P:(h + 1) * P], AQ[:, h // 2, 0:P], KZ[:, h, 0:P],
                                          start=True, stop=True)
                            for h in range(AT_HEADS):
                                ins = pe.matmul(ACC[:, 2 + h // 2, h % 2 * SEQ:(h % 2 + 1) * SEQ], AQ[:, h // 2, P:SEQ],
                                                KZ[:, h, :], start=True, stop=True)
                            ins.then_inc(qk_ps, 1)
                        if q == 9:
                            pe.wait_ge(pnorm, layer + 1)
                            for h in range(AT_HEADS):
                                pe.transpose(AUX[:, 0, h * P:(h + 1) * P], PA[:, h, :], ident[:, :])
                                for b in range(2):
                                    ins = pe.transpose(ACC[:, 2 + b, h * P:(h + 1) * P],
                                                       PB[:, h, b * P:(b + 1) * P], ident[:, :])
                            ins.then_inc(pT_ps, 1)
                        if q == 11:
                            pe.wait_ge(pT, layer * 2 + 2)
                            for h in range(AT_HEADS):
                                rows_ = slice(AT_DIM * (h % 2), AT_DIM * (h % 2) + AT_DIM)
                                to = AUX[rows_, 1, h // 2 * SEQ:(h // 2 + 1) * SEQ]
                                v = lambda b: AV[:, b, h * AT_DIM:(h + 1) * AT_DIM]
                                pe.matmul(to[:, 0:P], v(0), PTA[:, h, :], start=True, stop=True)
                                pe.matmul(to[:, P:SEQ], v(0), PTB[:, 0, h, :], start=True, stop=False)
                                ins = pe.matmul(to[:, P:SEQ], v(1), PTB[:, 1, h, :], start=False, stop=True)
                            ins.then_inc(at_ps, 1)
                    pe.wait_ge(level_out, layer * (NLV + 2) + NLV + 2)
                    pe.wait_ge(mix_lo, layer * 3 + 1)
                    pe.wait_ge(z_evac, layer * 10 + 9)
                    for h in range(HG_HEADS):
                        to = AUX[:, h // 2, h % 2 * SEQ:(h % 2 + 1) * SEQ]
                        v = lambda b: V[:, b, h * P:(h + 1) * P]
                        pe.matmul(to[:, 0:P], v(0), S[:, 2 * h, :], start=True, stop=True)
                        pe.matmul(to[:, P:SEQ], v(0), S10[:, h, :], start=True, stop=False)
                        ins = pe.matmul(to[:, P:SEQ], v(1), S[:, 2 * h + 1, :], start=False, stop=True)
                    ins.then_inc(o_ps, 1)
                    for o, kt in enumerate(OUT_ORDER):
                        if o == 2:
                            pe.wait_ge(o_sq, layer + 1)
                            pe.wait_ge(mix_f, layer * 2 + 1)
                            for a in range(2):
                                ins = pe.matmul(Z[:, a, :], ones[:, :], flat(D)[:, a * HALF:(a + 1) * HALF],
                                                start=True, stop=True)
                            ins.then_inc(ss_ps, 1)
                        if o % 2 == 0 and o <= 4:
                            pe.wait_ge(mix_lo, layer * 3 + o // 2 + 1)
                        down(mixT[:, :, kt, :], base + 2 * NPAIR + o, o == 0, o == KT - 1)

                pre(0)
                ffn(0)
                pre(1)
                mixer()
                pre(2)
                ffn(1)



INPUTS = ["x", "norm_w", "ffn1_wg", "ffn1_wu", "ffn1_wd", "mix_w_in", "mix_w_out", "hg_lb", "hg_norm_w", "conv_w",
          "ffn2_wg", "ffn2_wu", "ffn2_wd", "rel_bias"]


def kernel(**inputs):
    import numpy as np
    import concourse.bacc as bacc
    from concourse.bass_utils import run_bass_kernel_spmd

    nc = bacc.Bacc("TRN2", target_bir_lowering=False, num_devices=1)
    f32 = mybir.dt.float32
    arrays = {f"in_{n}": np.ascontiguousarray(inputs[n]) for n in INPUTS}
    arrays["in_dist_onehot"] = np.array([[float(bucket(SEQ - 1 - i) == b) for i in range(3 * P)]
                                         for b in range(BUCKETS)], np.float32)
    args = [nc.dram_tensor(n, a.shape, f32, kind="ExternalInput").ap() for n, a in arrays.items()]
    out = nc.dram_tensor("out_0", (1, SEQ, DM), f32, kind="ExternalOutput").ap()
    scratch = nc.dram_tensor("bias_scratch", (AT_HEADS, 3 * P), f32, kind="Internal").ap()
    trunk(nc, *args, out, scratch)
    r = run_bass_kernel_spmd(nc, [arrays], core_ids=[0])
    return r.results[0]["out_0"]
```

```python
from contextlib import ExitStack
import math

import concourse.bass as bass
from concourse import mybir

LAYERS, SEQ, DM, DFF = 2, 256, 1024, 2816
P = 128
TILES = SEQ // P
KT = DM // P
HG_HEADS, AT_HEADS, AT_DIM = 4, 4, 64
HG_WIDTH, AT_WIDTH, CV_WIDTH, TAPS = HG_HEADS * P, AT_HEADS * AT_DIM, 256, 3
BUCKETS, MAX_DIST = 32, 1024
EPS = 1e-6
NORMS = 6
SUB_FACTOR = (0.5, 1.0, 0.5)
FT = DFF // P
RING = 6
HALF = 512
FFN_UNITS = 3 * FT
W_IN_BLOCKS = {"hq": 0, "hf": 4, "hi": 8, "hg": 12, "aq": 16, "ak": 18, "av": 20, "cb": 22, "cc": 24, "ch": 26}
PAIRS = [("hi", 0), ("hi", 2), ("hf", 0), ("hf", 2), ("hq", 0), ("hq", 2), ("aq", 0), ("ak", 0), ("av", 0),
         ("cc", 0), ("ch", 0), ("cb", 0), ("hg", 0), ("hg", 2)]
OUT_ORDER = [6, 7, 4, 5, 0, 1, 2, 3]
NPAIR = len(PAIRS)
MIX_UNITS = 2 * NPAIR + KT
UNITS = 2 * FFN_UNITS + MIX_UNITS
FFN_BASE = [0, FFN_UNITS + MIX_UNITS]
MIX_BASE = FFN_UNITS
LEAD = 5
LEVELS = [64, 32, 16, 8, 4, 2, 1]
NLV = len(LEVELS)
FIRST_LEVEL_STEP = 5
FROM = 2
MASKED = -1e30
ACT_STEPS, DVE_STEPS, POOL_STEPS = 15, 117, 12
E_MAX = 2.0 ** 60


def bucket(dist):
    dist = max(dist, 0)
    exact = BUCKETS // 2
    if dist < exact:
        return dist
    return min(BUCKETS - 1, exact + int(math.log(dist / exact) / math.log(MAX_DIST / exact) * (BUCKETS - exact)))


class Count:

    def __init__(self, semaphore, *rounds):
        self.semaphore, self.rounds, self.n, self.loops = semaphore, rounds, 0, []

    def enter(self, register):
        self.loops.append((register, self.n))

    def leave(self, times):
        each = self.rounds[len(self.loops) - 1]
        _, before = self.loops.pop()
        assert self.n - before == each, (self.n - before, each)
        self.n = before + each * times

    def done(self, instruction):
        instruction.then_inc(self.semaphore, 1)
        self.n += 1

    def wait(self, engine):
        value = self.n
        for (register, _), each in zip(self.loops, self.rounds):
            value = register * each + value
        engine.wait_ge(self.semaphore, value)


def trunk(nc, x_in, norm_w, f1_wg, f1_wu, f1_wd, w_in, w_out, hg_lb, hg_nw, conv_w,
          f2_wg, f2_wu, f2_wd, rel_bias, dist_onehot, out, bias_scratch):
    f32, f32r, u32, i32 = mybir.dt.float32, mybir.dt.float32r, mybir.dt.uint32, mybir.dt.int32
    ALU, ACT, AX = mybir.AluOpType, mybir.ActivationFunctionType, mybir.AxisListType
    ffn_w = [(f1_wg, f1_wu, f1_wd), (f2_wg, f2_wu, f2_wd)]

    with ExitStack() as ctx:
        def sb(name, shape, dt=f32):
            return ctx.enter_context(nc.sbuf_tensor(name, shape, dt))

        def sem(name):
            return ctx.enter_context(nc.semaphore(name))

        raw = sb("raw", [P, RING, DM])
        wsp = sb("wsp", [P, RING, 2, DM], f32r)
        x = sb("x", [P, TILES, DM])
        nw = sb("nw", [P, 3, DM])
        xT = sb("xT", [P, 2, KT, SEQ], f32r)
        hT = sb("hT", [P, 2, 2, SEQ], f32r)
        mixT = sb("mixT", [P, 2, KT, SEQ], f32r)

        ident = sb("ident", [P, P])
        ones = sb("ones", [P, P])
        level_mask = sb("level_mask", [P, NLV, P // 2])
        keep = sb("keep", [P, HG_HEADS * TILES, P])
        bias = sb("bias", [P, AT_HEADS, 2 * P])
        relb = sb("relb", [BUCKETS, AT_HEADS])
        onehot = sb("onehot", [BUCKETS, 3 * P])
        brow = sb("brow", [AT_HEADS, 3 * P])
        lb_raw = sb("lb_raw", [P, LAYERS, HG_HEADS])
        lb_all = sb("lb_all", [P, LAYERS, 2 * HG_HEADS])
        lb_tmp = sb("lb_tmp", [P, 8, HG_HEADS])
        cw_all = sb("cw_all", [P, LAYERS, TAPS * 2])
        nw_all = sb("nw_all", [P, LAYERS])
        lb = sb("lb", [P, 2 * HG_HEADS])
        cw = sb("cw", [P, TAPS * 2])
        hnw = sb("hnw", [P, 1])
        eps4 = sb("eps4", [P, 1])
        minus_half = sb("minus_half", [P, 1])
        st = sb("st", [P, TILES, 8])
        spare = sb("spare", [P, 4])

        Q = sb("Q", [P, HG_HEADS, SEQ])
        B = sb("B", [P, HG_HEADS, SEQ])
        K = sb("K", [P, HG_HEADS, SEQ])
        D = sb("D", [P, HG_HEADS, SEQ])
        KL = sb("KL", [P, HG_HEADS, SEQ])
        QL = sb("QL", [P, HALF])
        S = sb("S", [P, HG_HEADS * TILES, P])
        S10 = sb("S10", [P, HG_HEADS, P])
        V = sb("V", [P, TILES, HG_WIDTH])
        G = sb("G", [P, HG_HEADS, SEQ])
        AQ = sb("AQ", [P, 2, SEQ])
        KZ = sb("KZ", [P, AT_HEADS, SEQ])
        AV = sb("AV", [P, TILES, AT_WIDTH])
        PA = sb("PA", [P, AT_HEADS, P])
        PB = sb("PB", [P, AT_HEADS, SEQ])
        PTA = sb("PTA", [P, AT_HEADS, P])
        PTB = sb("PTB", [P, 2, AT_HEADS, P])
        C = sb("C", [P, 2, SEQ])
        U = sb("U", [P, 2, SEQ + 2])
        Y = sb("Y", [P, 2, SEQ])
        smax = sb("smax", [P, 8])
        snmax = sb("snmax", [P, 8])
        ssum = sb("ssum", [P, 8])
        srec = sb("srec", [P, 8])
        xpose_of = lambda s, t: Z if t and s != 1 else AUX
        flat = lambda t: t[:, :, :].rearrange("p h t -> p (h t)")
        xn = [flat(D), flat(KL)]
        tmp = [flat(Q), flat(B)]
        junk = [flat(V), flat(G)]
        junk2 = [flat(PB), flat(K)]
        def level_exponents(engine, m, half):
            at = slice(half * HALF, (half + 1) * HALF)
            v = flat(B)[:, at].rearrange("p (g n) -> p g n", n=2 * m)
            return engine.tensor_tensor(flat(D)[:, at].rearrange("p (g n) -> p g n", n=2 * m), v,
                                        v[:, :, m - 1:m].broadcast_to([P, HALF // (2 * m), 2 * m]), ALU.subtract)

        hidden_of = lambda g: mixT[:, :, 0, :] if g == FT - 1 else hT[:, g % 2, :, :]
        ff = [flat(K)[:, 0:HALF], flat(K)[:, HALF:2 * HALF]]

        Z = ctx.enter_context(nc.psum_tensor("Z", [P, 2, HALF], f32))
        ACC = ctx.enter_context(nc.psum_tensor("ACC", [P, 4, HALF], f32))
        AUX = ctx.enter_context(nc.psum_tensor("AUX", [P, 2, HALF], f32))

        raw_loaded = [sem(f"raw_loaded{i}") for i in range(RING)]
        hi_done, split_done, unit_used = sem("hi_done"), sem("split_done"), sem("unit_used")
        lb_loaded, consts_loaded, x_loaded, onehot_loaded = sem("lb_loaded"), sem("consts_loaded"), sem("x_loaded"), sem("onehot_loaded")
        nw_loaded = [sem(f"nw_loaded{i}") for i in range(3)]
        pool_chain, consts_ready, bias_ready = sem("pool_chain"), sem("consts_ready"), sem("bias_ready")
        brow_ps, brow_sb, scratch_written, hankel_loaded = (
            sem("brow_ps"), sem("brow_sb"), sem("scratch_written"), sem("hankel_loaded"))
        lb_shifted, lb_exp = sem("lb_shifted"), sem("lb_exp")
        x_squared, acc_squared, x_rms, acc_rms, scaled, xn_ready, xpose_done, xhi_done, xlo_done = (
            sem("x_squared"), sem("acc_squared"), sem("x_rms"), sem("acc_rms"), sem("scaled"), sem("xn_ready"), sem("xpose_done"), sem("xhi_done"), sem("xlo_done"))
        start_ps, acc_ready, x_done = sem("start_ps"), sem("acc_ready"), sem("x_done")
        tanh_ready, z_free, h_ready = sem("tanh_ready"), sem("z_free"), sem("h_ready")
        act_chain, dve_chain = sem("act_chain"), sem("dve_chain")
        z_evac, e_clamped, logs_ready = sem("z_evac"), sem("e_clamped"), sem("logs_ready")
        exponents, decays, level_in, level_ps, level_out, k_ready, own_ps, own_out, b_ready, pool_exponents = (
            sem("exponents"), sem("decays"), sem("level_in"), sem("level_ps"), sem("level_out"), sem("k_ready"), sem("own_ps"), sem("own_out"), sem("b_ready"),
            sem("pool_exponents"))
        qk_ps, logits, probs, pnorm, pT_ps, pT, at_ps = (
            sem("qk_ps"), sem("logits"), sem("probs"), sem("pnorm"), sem("pT_ps"), sem("pT"), sem("at_ps"))
        gate_tanh, gate_done, conv_in, mix_f, mix_hi, mix_lo = (
            sem("gate_tanh"), sem("gate_done"), sem("conv_in"), sem("mix_f"), sem("mix_hi"), sem("mix_lo"))
        o_ps, o_sq, ss_ps, o_rs, out_done = sem("o_ps"), sem("o_sq"), sem("ss_ps"), sem("o_rs"), sem("out_done")

        block = ctx.enter_context(nc.Block())

        @block.sync
        def _(sp):
            def load(layer, u, src, more=0, rounds=0, slots=1):
                if u < RING and rounds == 0:
                    sp.wait_ge(split_done, layer * (UNITS + u - RING + 1) + FROM)
                else:
                    if slots:
                        sp.wait_ge(split_done, layer * UNITS + more + (u - RING + slots) + FROM)
                sp.dma_start(raw[:, u % RING, :].rearrange("p (k n) -> p k n", n=src.shape[-1]), src)\
                  .then_inc(raw_loaded[u % RING], 16)

            def cols(w, layer, c):
                n = w.shape[2]
                return bass.AP(tensor=w.tensor, offset=sp.snap(layer * (w.shape[1] * n) + c),
                               ap=[[n, P], [P * n, KT], [1, P]])

            def rows(w, layer, r):
                n = w.shape[2]
                return bass.AP(tensor=w.tensor, offset=sp.snap(layer * (w.shape[1] * n) + r * n),
                               ap=[[n, P], [P * n, 1], [1, n]])

            sp.dma_start(onehot[:, :], dist_onehot).then_inc(onehot_loaded, 16)
            sp.dma_start(relb[:, :], rel_bias).then_inc(onehot_loaded, 16)
            with sp.Fori(0, LAYERS) as layer:
                def ffn(f):
                    wg, wu, wd = ffn_w[f]
                    base = FFN_BASE[f]
                    load(layer, base + 0, cols(wg, layer, 0))
                    load(layer, base + 1, cols(wu, layer, 0))
                    load(layer, base + 2, cols(wg, layer, P))
                    load(layer, base + 3, cols(wu, layer, P))
                    load(layer, base + 4, rows(wd, layer, 0))
                    with sp.Fori(0, (FT - 4) // 2) as j:
                        for i in range(2):
                            at = (base + 5 + 3 * i)
                            load(layer, at, cols(wg, layer, j * (2 * P) + (2 + i) * P), j * RING, 1)
                            load(layer, at + 1, cols(wu, layer, j * (2 * P) + (2 + i) * P), j * RING, 1)
                            load(layer, at + 2, rows(wd, layer, j * (2 * P) + (1 + i) * P), j * RING, 1)
                    for i, (w, first) in enumerate(((wg, FT - 2), (wu, FT - 2), (wg, FT - 1), (wu, FT - 1))):
                        load(layer, base + FFN_UNITS - 7 + i, cols(w, layer, first * P))
                    for i in (3, 2):
                        load(layer, base + FFN_UNITS - i, rows(wd, layer, DFF - i * P))
                    load(layer, base + FFN_UNITS - 1, rows(wd, layer, DFF - P))

                ffn(0)
                starts = [(W_IN_BLOCKS[name] + first + c) * P for name, first in PAIRS for c in range(2)]
                starts += [kt * P for kt in OUT_ORDER] + [None]
                for i, start in enumerate(starts[:-1]):
                    load(layer, MIX_BASE + i, cols(w_in, layer, start) if i < 2 * NPAIR else rows(w_out, layer, start),
                         slots=0 if start == 0 else 2 if starts[i + 1] == 0 else 1)
                ffn(1)
            for t in range(TILES):
                sp.wait_ge(x_done, LAYERS * NORMS - TILES + t + 1 + FROM)
                sp.dma_start(out[0, t * P:(t + 1) * P, :], x[:, t, :]).then_inc(out_done, 16)
            sp.wait_ge(out_done, 16 * TILES)

        @block.gpsimd
        def _(pool):
            chain = Count(pool_chain, POOL_STEPS)

            def link(ins):
                chain.done(ins)
                chain.wait(pool)

            def norm_load(i, layer):
                row = norm_w[bass.ds(layer, 1), i:i + 1, :].rearrange("a b n -> (a b) n")
                pool.dma_start(nw[:, i % 3, :], row.broadcast_to([P, DM])).then_inc(nw_loaded[i % 3], 16)

            def norm_used(i, layer):
                if i % 2:
                    pool.wait_ge(x_done, layer * 6 + 2 * (i // 2) + 2 + FROM)
                else:
                    pool.wait_ge(xn_ready, layer * 12 + 4 * (i // 2) + 4 + FROM)

            def inverse_rms_x(s, layer, t):
                pool.wait_ge(x_squared, layer * 6 + 2 * s + t + 1)
                v = st[:, t, 2:3]
                link(pool.tensor_scalar(v, st[:, t, 0:1], EPS, None, ALU.add))
                pool.tensor_tensor(st[:, t, 3:4], v, minus_half[:, :], ALU.pow).then_inc(x_rms, 1)

            def inverse_rms_acc(s, layer, t):
                pool.wait_ge(acc_squared, layer * 12 + 4 * s + 2 * t + 2)
                v = st[:, t, 6:7]
                link(pool.tensor_scalar(v, st[:, t, 4:5], st[:, t, 5:6], EPS / SUB_FACTOR[s] ** 2, ALU.add, ALU.add))
                pool.tensor_tensor(st[:, t, 7:8], v, minus_half[:, :], ALU.pow).then_inc(acc_rms, 1)

            for i in range(2):
                norm_load(i, 0)
            link(pool.memset(ident[:, :], 0.0))
            link(pool.affine_select(out=ident[:, :], in_=ident[:, :], compare_op=ALU.not_equal, fill=1.0,
                                    base=0, pattern=[[-1, P]], channel_multiplier=1))
            link(pool.memset(minus_half[:, :], -0.5))
            pool.memset(eps4[:, :], 4 * EPS).then_inc(consts_ready, 1)
            for t in range(TILES):
                inverse_rms_x(0, 0, t)
            link(pool.memset(ones[:, :], 1.0))
            link(pool.memset(level_mask[:, :, :], 1.0))
            for n, m in enumerate(LEVELS):
                part = level_mask[:, n, :].rearrange("p (j m) -> p j m", m=m)
                link(pool.affine_select(out=part, in_=part, compare_op=ALU.is_ge, fill=0.0, base=0,
                                        pattern=[[-2 * m, P // (2 * m)], [0, m]], channel_multiplier=1))
                link(pool.affine_select(out=part, in_=part, compare_op=ALU.is_ge, fill=0.0, base=m - 1,
                                        pattern=[[2 * m, P // (2 * m)], [0, m]], channel_multiplier=-1))
            link(pool.memset(keep[:, :, :], 1.0))
            link(pool.memset(keep[:, :, 0:1], 0.0))
            link(pool.memset(KZ[:, :, :], 0.0))
            pool.memset(U[:, :, :], 0.0).then_inc(consts_ready, 1)
            pool.wait_ge(brow_sb, 1)
            pool.dma_start(bias_scratch, brow[:, :]).then_inc(scratch_written, 16)
            pool.wait_ge(scratch_written, 16)
            hankel = bass.AP(tensor=bias_scratch.tensor, offset=1, ap=[[1, P], [3 * P, AT_HEADS], [1, 2 * P]])
            rev = S[:, :, :].rearrange("p (h a) b -> p h (a b)", a=2)
            pool.dma_start(rev, hankel).then_inc(hankel_loaded, 16)
            pool.wait_ge(hankel_loaded, 16)
            link(pool.tensor_copy(bias[:, :, :], rev[:, :, ::-1]))
            pool.affine_select(out=bias[:, :, :], in_=bias[:, :, :], compare_op=ALU.is_ge, fill=MASKED, base=P,
                               pattern=[[0, AT_HEADS], [-1, 2 * P]], channel_multiplier=1).then_inc(bias_ready, 1)
            def norms(layer, following):
                for sub in range(3):
                    for i in (2 * sub - 1, 2 * sub):
                        if i + 3 < NORMS:
                            norm_used(i, layer)
                            norm_load(i + 3, layer)
                        elif following:
                            norm_used(i, layer)
                            norm_load(i + 3 - NORMS, layer + 1)
                    if sub == 1:
                        pool.wait_ge(b_ready, layer + 1)
                        for n, m in enumerate(LEVELS):
                            if n:
                                pool.wait_ge(level_in, layer * (NLV + 1) + n)
                            level_exponents(pool, m, 0).then_inc(pool_exponents, 1)
                    if sub == 0:
                        for t in range(TILES):
                            inverse_rms_acc(sub, layer, t)
                            inverse_rms_x(sub + 1, layer, t)
                    else:
                        for t in range(TILES):
                            inverse_rms_acc(sub, layer, t)
                        for t in range(TILES):
                            if sub == 1:
                                inverse_rms_x(sub + 1, layer, t)
                            elif following:
                                inverse_rms_x(0, layer + 1, t)

            with pool.Fori(0, LAYERS - 1) as layer:
                chain.enter(layer)
                norms(layer, True)
                chain.leave(LAYERS - 1)
            norms(LAYERS - 1, False)
            for i in range(3):
                pool.wait_ge(nw_loaded[i], 16 * 2 * LAYERS)

        @block.scalar
        def _(act):
            chain = Count(act_chain, ACT_STEPS)

            act.dma_start(lb_raw[:, :, :], hg_lb.rearrange("l (h p) -> p l h", p=P),
                          allow_slow_non_contiguous=True).then_inc(lb_loaded, 16)
            act.dma_start(x[:, :, :], x_in[0].rearrange("(t p) n -> p t n", p=P)).then_inc(x_loaded, 16)
            act.dma_start(cw_all[:, :, :].rearrange("p l (w c) -> p (l w) c", c=2),
                          conv_w.rearrange("l w (c p) -> p (l w) c", p=P), allow_slow_non_contiguous=True).then_inc(consts_loaded, 16)
            act.dma_start(nw_all[:, :], hg_nw.rearrange("l p -> p l"), allow_slow_non_contiguous=True).then_inc(consts_loaded, 16)

            act.wait_ge(lb_shifted, 1)
            act.activation(lb_tmp[:, 1:3, :], lb_tmp[:, 1:3, :], ACT.Exp).then_inc(lb_exp, 1)
            act.wait_ge(x_loaded, 16)
            act.wait_ge(consts_ready, 1)

            with act.Fori(0, LAYERS) as layer:
                chain.enter(layer)

                def U_(u, more=0):
                    return layer * UNITS + more + u

                def split(u, more=0, rounds=0):
                    act.wait_ge(raw_loaded[u % RING], (layer * (UNITS // RING) + rounds + (u // RING + 1)) * 16)
                    act.wait_ge(unit_used, (layer * UNITS if u < RING else U_(u - RING + 1, more)) + FROM)
                    act.activation(wsp[:, u % RING, 0, :], raw[:, u % RING, :], ACT.Copy).then_inc(hi_done, 1)

                def squares_x(s, t):
                    act.wait_ge(x_done, layer * NORMS + 2 * s + t - 1 + FROM)
                    act.activation(junk[t], x[:, t, :], ACT.Square, scale=DM ** -0.5, accum_out=st[:, t, 0:1])\
                       .then_inc(x_squared, 1)

                def squares_acc(s, t, h):
                    if h:
                        act.wait_ge(scaled, layer * 12 + 4 * s + 2 * t + 1)
                    elif t == 0:
                        act.wait_ge(acc_ready, layer * 3 + s + 1)
                    else:
                        act.wait_ge(unit_used, U_((FFN_UNITS, FFN_BASE[1], UNITS)[s]) + FROM)
                    act.activation(junk2[t][:, h * HALF:(h + 1) * HALF], ACC[:, 2 * t + h, :], ACT.Square,
                                   scale=DM ** -0.5 / SUB_FACTOR[s], accum_out=st[:, t, 4 + h:5 + h])\
                       .then_inc(acc_squared, 1)

                def high(s, t):
                    for h in range(2):
                        act.wait_ge(xpose_done, layer * 12 + 4 * s + 2 * t + h + 1)
                        act.activation(xT[:, 0, 4 * h:4 * h + 4, t * P:(t + 1) * P],
                                       xpose_of(s, t)[:, h, :].rearrange("p (k n) -> p k n", k=4), ACT.Copy)\
                           .then_inc(xhi_done, 1)

                def pre(s, fills):
                    for t in range(TILES):
                        squares_x(s, t)
                    for u in fills[0]:
                        split(u)
                    for t in range(TILES):
                        high(s, t)
                        for u in fills[1 + t]:
                            split(u)

                def post(s):
                    squares_acc(s, 0, 0)
                    squares_acc(s, 0, 1)
                    squares_acc(s, 1, 0)
                    if s == 0:
                        squares_x(1, 0)
                        squares_acc(s, 1, 1)
                        high(1, 0)
                        split(MIX_BASE + LEAD - 1)
                        squares_x(1, 1)
                        high(1, 1)
                    else:
                        squares_acc(s, 1, 1)

                def ffn(f):
                    base = FFN_BASE[f]

                    def gate(g, more=0):
                        used = 2 if g == 0 else 3 * g if g == FT - 1 else 3 * g + 1
                        act.wait_ge(unit_used, U_(base + used, more) + FROM)
                        act.activation(ff[g % 2][:, 0:SEQ], Z[:, g % 2, 0:SEQ], ACT.Tanh, scale=0.5)\
                           .then_inc(tanh_ready, 1)

                    for g in range(2):
                        gate(g)
                        for i in range(3):
                            split(base + LEAD + 3 * g + i)
                    with act.Fori(0, (FT - 4) // 2) as j:
                        for g in range(2, 4):
                            gate(g, j * RING)
                            for i in range(3):
                                split(base + LEAD + 3 * g + i, j * RING, j)
                    last = FT - 2
                    gate(last)
                    split(base + FFN_UNITS - 1)
                    if f == 0:
                        split(base + FFN_UNITS)
                    gate(last + 1)
                    if f == 0:
                        for i in range(1, LEAD - 1):
                            split(base + FFN_UNITS + i)

                def mixer():
                    base = MIX_BASE

                    def evac(p, dst, src):
                        act.activation(dst, src, ACT.Copy).then_inc(z_evac, 1)

                    for q in range(NPAIR + KT // 2):
                        split(base + LEAD + 2 * q)
                        if q == 13:
                            act.wait_ge(at_ps, layer + 1)
                            act.activation(mixT[:, 0, 4:6, :], AUX[:, 1, :].rearrange("p (a t) -> p a t", a=2),
                                           ACT.Copy).then_inc(mix_hi, 1)
                        if q < NPAIR:
                            if q == 0:
                                act.wait_ge(start_ps, layer + 1)
                            else:
                                act.wait_ge(unit_used, U_(base + 2 * q + 2) + FROM)
                            z = Z[:, q % 2, :]
                            name, first = PAIRS[q]
                            two = z.rearrange("p (h t) -> p h t", h=2)
                            if name == "hf":
                                act.activation(K[:, first:first + 2, :], two, ACT.Exp, scale=-1.0).then_inc(z_evac, 1)
                            elif name == "hq":
                                evac(q, Q[:, first:first + 2, :], two)
                            elif name == "aq":
                                evac(q, AQ[:, :, :], two)
                            elif name == "ak":
                                chain.done(act.activation(KZ[0:AT_DIM, 0:4:2, :], two[0:AT_DIM, :, :], ACT.Copy))
                                evac(q, KZ[AT_DIM:P, 1:4:2, :], two[AT_DIM:P, :, :])
                            elif name == "av":
                                evac(q, AV[:, :, :], two)
                            elif name == "hi":
                                evac(q, V[:, q, :], z)
                            elif name == "hg":
                                act.activation(G[:, first:first + 2, :], two, ACT.Tanh, scale=0.5)\
                                   .then_inc(gate_tanh, 1)
                            elif name == "cc":
                                evac(q, C[:, :, :], two)
                        if q == 3:
                            split(base + LEAD + 2 * q + 1)
                            act.wait_ge(e_clamped, layer + 1)
                            chain.done(act.activation(flat(D), flat(K), ACT.Ln, bias=1.0))
                            for h in range(HG_HEADS):
                                chain.done(act.activation(B[:, h, :], K[:, h, :], ACT.Ln, bias=1.0,
                                                          scale=lb[:, h:h + 1]))
                            chain.wait(act)
                            act.activation(flat(KL), flat(D), ACT.Exp, scale=-1.0).then_inc(logs_ready, 1)
                        n = q - FIRST_LEVEL_STEP
                        if 0 <= n <= NLV:
                            act.wait_ge(exponents, layer * (NLV + 1) + n + 1)
                            if n < NLV:
                                act.wait_ge(pool_exponents, layer * NLV + n + 1)
                            if n < NLV:
                                v = flat(D).rearrange("p (g q m) -> p g q m", q=2, m=LEVELS[n])
                                chain.done(act.activation(v[:, :, 0, :], v[:, :, 0, :], ACT.Exp, scale=-1.0))
                                act.activation(v[:, :, 1, :], v[:, :, 1, :], ACT.Exp).then_inc(decays, 1)
                            else:
                                chain.done(act.activation(D[:, :, 0:P], D[:, :, 0:P], ACT.Exp, scale=-1.0))
                                act.activation(D[:, :, P:SEQ], B[:, :, P:SEQ], ACT.Exp).then_inc(decays, 1)
                        if q == 11:
                            act.wait_ge(pT_ps, layer + 1)
                            act.activation(PTA[:, :, :], AUX[:, 0, :].rearrange("p (h t) -> p h t", h=4), ACT.Copy)\
                               .then_inc(pT, 1)
                            act.activation(PTB[:, :, :, :].rearrange("p a h t -> p a (h t)"), ACC[:, 2:4, :], ACT.Copy)\
                               .then_inc(pT, 1)
                        if q != 3 and q < NPAIR + KT // 2 - 1:
                            split(base + LEAD + 2 * q + 1)
                        if q == 8:
                            act.wait_ge(logits, layer + 1)
                            for h in range(AT_HEADS):
                                act.activation(PA[:, h, :], PA[:, h, :], ACT.Exp, bias=snmax[:, h:h + 1],
                                               accum_out=ssum[:, h:h + 1]).then_inc(probs, 1)
                                act.activation(PB[:, h, :], PB[:, h, :], ACT.Exp, bias=snmax[:, 4 + h:5 + h],
                                               accum_out=ssum[:, 4 + h:5 + h]).then_inc(probs, 1)
                        if q == 11:
                            act.wait_ge(mix_f, layer * 2 + 1)
                            act.activation(mixT[:, 0, 6:8, :], Y[:, :, :], ACT.Copy).then_inc(mix_hi, 1)
                        if q == NPAIR - 1:
                            act.wait_ge(o_ps, layer + 1)
                            act.activation(flat(D), AUX[:, :, :].rearrange("p a b -> p (a b)"), ACT.Square)\
                               .then_inc(o_sq, 1)
                        if q == NPAIR:
                            act.wait_ge(ss_ps, layer + 1)
                            chain.done(act.activation(flat(K), Z[:, :, :].rearrange("p a b -> p (a b)"), ACT.Ln,
                                                      bias=eps4[:, :], scale=4.0 / P))
                            chain.wait(act)
                            act.activation(flat(K), flat(K), ACT.Exp, scale=-0.5).then_inc(o_rs, 1)
                        if q == NPAIR + 1:
                            act.wait_ge(mix_f, layer * 2 + 2)
                            act.activation(mixT[:, 0, 0:4, :], Q[:, :, :], ACT.Copy).then_inc(mix_hi, 1)

                pre(0, ([0], [1], [2, 3, 4]))
                ffn(0)
                post(0)
                mixer()
                post(1)
                pre(2, ([], [], [FFN_BASE[1] + LEAD - 1]))
                ffn(1)
                post(2)
                chain.leave(LAYERS)

        @block.vector
        def _(dve):
            chain = Count(dve_chain, DVE_STEPS, 4)

            def link(ins):
                chain.done(ins)
                chain.wait(dve)

            for i, started in enumerate((split_done, xn_ready, x_done)):
                dve.memset(spare[:, i:i + 1], 0.0).then_inc(started, FROM)
            dve.wait_ge(lb_loaded, 16)
            a = [lb_raw[:, l, :] for l in range(LAYERS)]
            mx, e0, e1, tot, rec, s0, s1, cum = [lb_tmp[:, i, :] for i in range(8)]
            link(dve.tensor_tensor(mx, a[0], a[1], ALU.max))
            link(dve.tensor_tensor(e0, a[0], mx, ALU.subtract))
            dve.tensor_tensor(e1, a[1], mx, ALU.subtract).then_inc(lb_shifted, 1)
            dve.wait_ge(lb_exp, 1)
            link(dve.tensor_tensor(tot, e0, e1, ALU.add))
            link(dve.reciprocal(rec, tot))
            link(dve.tensor_tensor(s0, e0, rec, ALU.mult))
            link(dve.tensor_tensor(s1, e1, rec, ALU.mult))
            link(dve.tensor_tensor(cum, s0, s1, ALU.add))
            link(dve.tensor_tensor(lb_all[:, 0, 0:HG_HEADS], s0, s0, ALU.subtract))
            link(dve.tensor_tensor(lb_all[:, 1, 0:HG_HEADS], cum, s0, ALU.subtract))
            link(dve.tensor_scalar(lb_all[:, :, HG_HEADS:], lb_all[:, :, 0:HG_HEADS], -1.0, 1.0, ALU.mult, ALU.add))
            dve.wait_ge(brow_ps, 1)
            dve.tensor_copy(brow[:, :], AUX[0:AT_HEADS, 0, 0:3 * P]).then_inc(brow_sb, 1)

            with dve.Fori(0, LAYERS) as layer:
                chain.enter(layer)

                def U_(u, more=0):
                    return layer * UNITS + more + u

                def split(u, more=0):
                    dve.wait_ge(hi_done, U_(u + 1, more))
                    dve.tensor_tensor(wsp[:, u % RING, 1, :], raw[:, u % RING, :],
                                      wsp[:, u % RING, 0, :].bitcast(f32), ALU.subtract).then_inc(split_done, 1)

                def weights_of(i):
                    dve.wait_ge(nw_loaded[i % 3], (layer * 2 + (i // 3 + 1)) * 16)
                    return nw[:, i % 3, :]

                def normed(s, t):
                    w = weights_of(2 * s)
                    dve.wait_ge(x_rms, layer * 6 + 2 * s + t + 1)
                    for h in range(2):
                        half = slice(h * HALF, (h + 1) * HALF)
                        dve.scalar_tensor_tensor(xn[t][:, half], x[:, t, half], st[:, t, 3:4], w[:, half],
                                                 ALU.mult, ALU.mult).then_inc(xn_ready, 1)

                def low(s, t):
                    at = slice(t * P, (t + 1) * P)
                    for h in range(2):
                        dve.wait_ge(xhi_done, layer * 12 + 4 * s + 2 * t + h + 1)
                        dve.tensor_tensor(xT[:, 1, 4 * h:4 * h + 4, at],
                                          xpose_of(s, t)[:, h, :].rearrange("p (k n) -> p k n", k=4),
                                          xT[:, 0, 4 * h:4 * h + 4, at].bitcast(f32), ALU.subtract)\
                           .then_inc(xlo_done, 1)

                def pre(s, fills):
                    normed(s, 0)
                    for u in fills[0]:
                        split(u)
                    normed(s, 1)
                    for t in range(TILES):
                        low(s, t)
                        for u in fills[1 + t]:
                            split(u)

                def post(s):
                    w = weights_of(2 * s + 1)

                    def scale(t):
                        if t == 0:
                            dve.wait_ge(acc_ready, layer * 3 + s + 1)
                        else:
                            dve.wait_ge(unit_used, U_((FFN_UNITS, FFN_BASE[1], UNITS)[s]) + FROM)
                        for h in (1, 0):
                            if h == 0:
                                dve.wait_ge(acc_squared, layer * 12 + 4 * s + 2 * t + 1)
                            half = slice(h * HALF, (h + 1) * HALF)
                            dve.tensor_tensor(tmp[t][:, half], ACC[:, 2 * t + h, :], w[:, half], ALU.mult)\
                               .then_inc(scaled, 1)

                    def add(t):
                        dve.wait_ge(scaled, layer * 12 + 4 * s + 2 * t + 2)
                        dve.wait_ge(acc_rms, layer * 6 + 2 * s + t + 1)
                        dve.scalar_tensor_tensor(x[:, t, :], tmp[t], st[:, t, 7:8], x[:, t, :], ALU.mult, ALU.add)\
                           .then_inc(x_done, 1)

                    scale(0)
                    if s == 0:
                        add(0)
                        scale(1)
                        normed(1, 0)
                        add(1)
                        low(1, 0)
                        split(MIX_BASE + LEAD - 1)
                        normed(1, 1)
                        low(1, 1)
                    else:
                        scale(1)
                        add(0)
                        add(1)

                def ffn(f):
                    base = FFN_BASE[f]

                    def hidden(g, more=0, rounds=0):
                        dve.wait_ge(tanh_ready, layer * (2 * FT) + rounds + (FT * f + g + 1))
                        e, h = ff[g % 2][:, 0:SEQ], ff[g % 2][:, SEQ:2 * SEQ]
                        link(dve.scalar_tensor_tensor(e, e, 1.0, Z[:, g % 2, 0:SEQ], ALU.add, ALU.mult))
                        link(dve.scalar_tensor_tensor(h, e, 0.5, Z[:, g % 2, SEQ:2 * SEQ], ALU.mult, ALU.mult))
                        to = hidden_of(g)
                        if 2 <= g < FT - 1:
                            dve.wait_ge(unit_used, U_(base + 4 + 3 * (g - 2) + 1, more) + FROM)
                        dve.tensor_copy(to[:, 0, :], h).then_inc(z_free, 1)
                        dve.wait_ge(z_free, layer * (2 * FT) + rounds + (FT * f + g + 1))
                        dve.tensor_tensor(to[:, 1, :], h, to[:, 0, :].bitcast(f32), ALU.subtract)\
                           .then_inc(h_ready, 1)

                    for g in range(2):
                        hidden(g)
                        for i in range(3):
                            split(base + LEAD + 3 * g + i)
                    with dve.Fori(0, (FT - 4) // 2) as j:
                        chain.enter(j)
                        for g in range(2, 4):
                            hidden(g, j * RING, j * 2)
                            for i in range(3):
                                split(base + LEAD + 3 * g + i, j * RING)
                        chain.leave((FT - 4) // 2)
                    last = FT - 2
                    hidden(last)
                    split(base + FFN_UNITS - 1)
                    if f == 0:
                        split(base + FFN_UNITS)
                    hidden(last + 1)
                    if f == 0:
                        for i in range(1, LEAD - 1):
                            split(base + FFN_UNITS + i)

                def mixer():
                    base = MIX_BASE
                    z_of = lambda q: Z[:, q % 2, :].rearrange("p (h t) -> p h t", h=2)
                    dve.wait_ge(consts_ready, 2)
                    dve.wait_ge(consts_loaded, 32)
                    chain.done(dve.tensor_copy(lb[:, :], lb_all[:, bass.ds(layer, 1), :].rearrange("p a n -> p (a n)")))
                    chain.done(dve.tensor_copy(cw[:, :], cw_all[:, bass.ds(layer, 1), :].rearrange("p a n -> p (a n)")))
                    link(dve.tensor_copy(hnw[:, :], nw_all[:, bass.ds(layer, 1)]))
                    dve.wait_ge(bias_ready, 1)
                    link(dve.memset(S[:, :, :], 0.0))
                    for q in range(NPAIR + KT // 2):
                        if q == 3:
                            dve.wait_ge(z_evac, layer * 10 + 4)
                            dve.tensor_scalar(flat(K), flat(K), E_MAX, None, ALU.min).then_inc(e_clamped, 1)
                        if q == 4:
                            dve.wait_ge(logs_ready, layer + 1)
                            chain.done(dve.tensor_tensor(flat(B), flat(B), flat(D), ALU.subtract))
                            for h in range(HG_HEADS):
                                ins = dve.scalar_tensor_tensor(K[:, h, :], K[:, h, :], lb[:, HG_HEADS + h:HG_HEADS + h + 1],
                                                               KL[:, h, :], ALU.mult, ALU.mult)
                                if h < HG_HEADS - 1:
                                    chain.done(ins)
                            ins.then_inc(k_ready, 1)
                            chain.wait(dve)
                            dve.tensor_tensor_scan(flat(B), keep[:, :, :].rearrange("p g t -> p (g t)"), flat(B),
                                                   0.0, ALU.mult, ALU.add).then_inc(b_ready, 1)
                            dve.wait_ge(b_ready, layer + 1)
                        n = q - FIRST_LEVEL_STEP
                        if 1 <= n <= NLV:
                            dve.wait_ge(level_in, layer * (NLV + 1) + n)
                        if 0 <= n < NLV:
                            m = LEVELS[n]
                            level_exponents(dve, m, 1).then_inc(exponents, 1)
                        if n == NLV:
                            dve.tensor_tensor(D[:, :, 0:P], B[:, :, 0:P],
                                              B[:, :, P - 1:P].broadcast_to([P, HG_HEADS, P]), ALU.subtract)\
                               .then_inc(exponents, 1)
                        split(base + LEAD + 2 * q)
                        if q == 13:
                            dve.wait_ge(mix_hi, layer * 3 + 2)
                            dve.tensor_tensor(mixT[:, 1, 4:6, :], AUX[:, 1, :].rearrange("p (a t) -> p a t", a=2),
                                              mixT[:, 0, 4:6, :].bitcast(f32), ALU.subtract).then_inc(mix_lo, 1)
                        if q < 5:
                            split(base + LEAD + 2 * q + 1)
                        if 0 <= n <= NLV:
                            dve.wait_ge(decays, layer * (NLV + 1) + n + 1)
                            dve.wait_ge(z_evac, layer * 10 + 6)
                            if n:
                                dve.wait_ge(level_ps, layer * (NLV + 1) + n)
                            if n < NLV:
                                by = lambda t: flat(t).rearrange("p (g q m) -> p g q m", q=2, m=LEVELS[n])
                                chain.done(dve.tensor_tensor(by(KL)[:, :, 0, :], by(K)[:, :, 0, :], by(D)[:, :, 0, :],
                                                             ALU.mult))
                                dve.tensor_tensor(QL[:, :].rearrange("p (g m) -> p g m", m=LEVELS[n]),
                                                  by(Q)[:, :, 1, :], by(D)[:, :, 1, :], ALU.mult).then_inc(level_in, 1)
                            else:
                                chain.done(dve.tensor_tensor(KL[:, :, 0:P], K[:, :, 0:P], D[:, :, 0:P], ALU.mult))
                                dve.tensor_tensor(QL[:, :].rearrange("p (g m) -> p g m", m=P),
                                                  Q[:, :, P:SEQ], D[:, :, P:SEQ], ALU.mult).then_inc(level_in, 1)
                        if 5 <= q < NPAIR - 1:
                            split(base + LEAD + 2 * q + 1)
                        if q == FIRST_LEVEL_STEP + 1:
                            dve.wait_ge(own_ps, layer + 1)
                            mask = ident[:, :].bitcast(u32).rearrange("p (g t) -> p g t", g=1).broadcast_to([P, 8, P])
                            dve.memset(spare[:, 3:4], 0.0)
                            dve.copy_predicated(S[:, :, :], mask, ACC[:, 2:4, :].rearrange(
                                "p a (g t) -> p (a g) t", t=P)).then_inc(own_out, 1)
                            dve.wait_ge(own_out, layer + 1)
                        c = n - 1
                        if 0 <= c <= NLV:
                            dve.wait_ge(level_ps, layer * (NLV + 1) + c + 1)
                            if c:
                                dve.wait_ge(level_out, layer * (NLV + 1) + c)
                            if c < NLV:
                                m = LEVELS[c]
                                into = S[:, :, :].rearrange("p g (j q m) -> p g j q m", q=2, m=m)[:, :, :, 1, :]
                                mask = level_mask[:, c, :].bitcast(u32).rearrange("p (g j m) -> p g j m", g=1, m=m)\
                                    .broadcast_to([P, 8, P // (2 * m), m])
                                dve.memset(spare[:, 3:4], 0.0)
                                dve.copy_predicated(into, mask, ACC[:, c % 2, :].rearrange(
                                    "p (g j m) -> p g j m", g=8, m=m)).then_inc(level_out, 1)
                            else:
                                dve.tensor_copy(S10[:, :, :], ACC[:, NLV % 2, :].rearrange("p (h t) -> p h t", h=4))\
                                   .then_inc(level_out, 1)
                        if NPAIR - 1 <= q < NPAIR + KT // 2 - 1:
                            split(base + LEAD + 2 * q + 1)
                        if q == 8:
                            dve.wait_ge(qk_ps, layer + 1)
                            scale = float(AT_DIM) ** -0.5
                            chain.done(dve.scalar_tensor_tensor(
                                PA[:, :, :], AUX[:, 0, :].rearrange("p (h t) -> p h t", h=4), scale,
                                bias[:, :, P:2 * P], ALU.mult, ALU.add))
                            link(dve.scalar_tensor_tensor(
                                PB[:, :, :], ACC[:, 2:4, :].rearrange("p a (h t) -> p (a h) t", t=SEQ), scale,
                                bias[:, :, :], ALU.mult, ALU.add))
                            chain.done(dve.reduce_max(smax[:, 0:4], PA[:, :, :], AX.X))
                            link(dve.reduce_max(smax[:, 4:8], PB[:, :, :], AX.X))
                            dve.tensor_scalar(snmax[:, :], smax[:, :], -1.0, None, ALU.mult).then_inc(logits, 1)
                        if q == 9:
                            dve.wait_ge(probs, layer * 8 + 8)
                            link(dve.reciprocal(srec[:, :], ssum[:, :]))
                            chain.done(dve.tensor_tensor(PA[:, :, :], PA[:, :, :], srec[:, 0:4].rearrange(
                                "p (h a) -> p h a", a=1).broadcast_to([P, 4, P]), ALU.mult))
                            dve.tensor_tensor(PB[:, :, :], PB[:, :, :], srec[:, 4:8].rearrange(
                                "p (h a) -> p h a", a=1).broadcast_to([P, 4, SEQ]), ALU.mult).then_inc(pnorm, 1)
                        if q < NPAIR and PAIRS[q][0] == "hg":
                            first = PAIRS[q][1]
                            part = G[:, first:first + 2, :]
                            dve.wait_ge(gate_tanh, layer * 2 + first // 2 + 1)
                            dve.scalar_tensor_tensor(part, part, 1.0, z_of(q), ALU.add, ALU.mult).then_inc(gate_done, 1)
                        if q == 10:
                            dve.wait_ge(z_evac, layer * 10 + 10)
                            dve.wait_ge(unit_used, U_(base + 2 * q + 2) + FROM)
                            dve.tensor_tensor(U[:, :, 2:], z_of(q), C[:, :, :], ALU.mult).then_inc(conv_in, 1)
                            dve.wait_ge(conv_in, layer + 1)
                            tap = lambda i, c_: cw[:, 2 * i + c_:2 * i + c_ + 1]
                            for c_ in range(2):
                                chain.done(dve.tensor_scalar(Y[:, c_, :], U[:, c_, 2:], tap(2, c_), None, ALU.mult))
                            for i in (1, 0):
                                chain.wait(dve)
                                for c_ in range(2):
                                    chain.done(dve.scalar_tensor_tensor(Y[:, c_, :], U[:, c_, i:i + SEQ], tap(i, c_),
                                                                        Y[:, c_, :], ALU.mult, ALU.add))
                            chain.wait(dve)
                        if q == 11:
                            dve.wait_ge(unit_used, U_(base + 2 * q + 2) + FROM)
                            dve.tensor_tensor(Y[:, :, :], z_of(q), Y[:, :, :], ALU.mult).then_inc(mix_f, 1)
                        if q == 12:
                            dve.wait_ge(mix_hi, layer * 3 + 1)
                            dve.tensor_tensor(mixT[:, 1, 6:8, :], Y[:, :, :], mixT[:, 0, 6:8, :].bitcast(f32),
                                              ALU.subtract).then_inc(mix_lo, 1)
                        if q == NPAIR - 1:
                            dve.wait_ge(gate_done, layer * 2 + 2)
                            dve.wait_ge(o_sq, layer + 1)
                            link(dve.scalar_tensor_tensor(flat(Q), AUX[:, :, :].rearrange("p a b -> p (a b)"),
                                                          hnw[:, :], flat(G), ALU.mult, ALU.mult))
                        if q == NPAIR + 1 - 1:
                            dve.wait_ge(o_rs, layer + 1)
                            dve.tensor_tensor(flat(Q), flat(Q), flat(K), ALU.mult).then_inc(mix_f, 1)
                        if q == NPAIR + 1:
                            dve.wait_ge(mix_hi, layer * 3 + 3)
                            dve.tensor_tensor(mixT[:, 1, 0:4, :], Q[:, :, :], mixT[:, 0, 0:4, :].bitcast(f32),
                                              ALU.subtract).then_inc(mix_lo, 1)

                pre(0, ([0], [1], [2, 3, 4]))
                ffn(0)
                post(0)
                mixer()
                post(1)
                pre(2, ([], [], [FFN_BASE[1] + LEAD - 1]))
                ffn(1)
                post(2)
                chain.leave(LAYERS)

        @block.tensor
        def _(pe):
            pe.wait_ge(onehot_loaded, 32)
            pe.matmul(AUX[0:AT_HEADS, 0, 0:P], relb[:, :], onehot[:, 0:P], start=True, stop=True)\
              .then_inc(unit_used, FROM)
            pe.matmul(AUX[0:AT_HEADS, 0, P:3 * P], relb[:, :], onehot[:, P:3 * P], start=True, stop=True)\
              .then_inc(brow_ps, 1)
            pe.wait_ge(consts_ready, 1)

            PRODUCTS = ((0, 0), (0, 1), (1, 0))

            with pe.Fori(0, LAYERS) as layer:
                def U_(u, more=0):
                    return layer * UNITS + more + u

                def feature_major(dst, u, more=0, normed=None):
                    pe.wait_ge(split_done, U_(u + 1, more) + FROM)
                    for k in range(KT):
                        if normed is not None and k % 4 == 0:
                            pe.wait_ge(xlo_done, layer * 12 + 4 * normed + 3 + k // 4)
                        for a, b in PRODUCTS:
                            ins = pe.matmul(dst, wsp[:, u % RING, a, k * P:(k + 1) * P], xT[:, b, k, :],
                                            start=(k == 0 and a + b == 0), stop=(k == KT - 1 and a == 1))
                    ins.then_inc(unit_used, 1)

                def token_major(dst, t, u, units, ks=range(KT)):
                    pe.wait_ge(split_done, U_(u + units) + FROM)
                    s = u % RING
                    for k in ks:
                        for a, b in PRODUCTS:
                            ins = pe.matmul(dst.rearrange("p (c n) -> p c n", c=units),
                                            xT[:, b, k, t * P:(t + 1) * P], wsp[:, s:s + units, a, k * P:(k + 1) * P],
                                            start=(k == 0 and a + b == 0), stop=(k == KT - 1 and a == 1))
                    return ins

                def down_tile(left, u, t, first, last, more=0):
                    for a, b in PRODUCTS:
                        for h in range(2):
                            ins = pe.matmul(ACC[:, 2 * t + h, :], left[:, b, t * P:(t + 1) * P],
                                            wsp[:, u % RING, a, h * HALF:(h + 1) * HALF],
                                            start=(first and a + b == 0), stop=(last and a == 1))
                    return ins

                def down(left, u, first, more=0):
                    pe.wait_ge(split_done, U_(u + 1, more) + FROM)
                    down_tile(left, u, 0, first, False)
                    down_tile(left, u, 1, first, False).then_inc(unit_used, 1)

                def down_last(lefts, u, ready):
                    for i in range(2):
                        pe.wait_ge(split_done, U_(u + i + 1) + FROM)
                        if ready:
                            pe.wait_ge(*ready[i])
                        ins = down_tile(lefts[i], u + i, 0, False, i == 1)
                    ins.then_inc(acc_ready, 1)
                    for i in range(2):
                        down_tile(lefts[i], u + i, 1, False, i == 1).then_inc(unit_used, 1)

                def transposes(s, t):
                    for h in range(2):
                        pe.wait_ge(xn_ready, layer * 12 + 4 * s + 2 * t + h + 1 + FROM)
                        if t and s == 1:
                            pe.wait_ge(xlo_done, layer * 12 + 4 * s + h + 1)
                        for k in range(4):
                            ins = pe.transpose(xpose_of(s, t)[:, h, k * P:(k + 1) * P],
                                               xn[t][:, (4 * h + k) * P:(4 * h + k + 1) * P], ident[:, :])
                        ins.then_inc(xpose_done, 1)

                def pre_and_first_units(s, u):
                    transposes(s, 0)
                    pe.wait_ge(xlo_done, layer * 12 + 4 * s + 1)
                    token_major(Z[:, 0, :], 0, u, 4, range(KT // 2))
                    pe.wait_ge(xlo_done, layer * 12 + 4 * s + 2)
                    transposes(s, 1)
                    token_major(Z[:, 0, :], 0, u, 4, range(KT // 2, KT)).then_inc(start_ps, 1)
                    pe.wait_ge(xlo_done, layer * 12 + 4 * s + 4)
                    token_major(Z[:, 1, :], 1, u, 4).then_inc(unit_used, 4)

                def ffn(f):
                    base = FFN_BASE[f]

                    def gate_up(g, u, more=0, rounds=0):
                        if g >= 2:
                            pe.wait_ge(z_free, layer * (2 * FT) + rounds + (FT * f + g - 1))
                        feature_major(Z[:, g % 2, 0:SEQ], u, more, 2 * f if g == 0 else None)
                        feature_major(Z[:, g % 2, SEQ:2 * SEQ], u + 1, more)

                    def ready(g, rounds=0):
                        return h_ready, layer * (2 * FT) + rounds + (FT * f + g + 1)

                    def down_of(g, u, more=0, rounds=0, first=False):
                        pe.wait_ge(*ready(g, rounds))
                        down(hidden_of(g), u, first, more)

                    for t in range(TILES):
                        transposes(2 * f, t)
                    gate_up(0, base)
                    gate_up(1, base + 2)
                    down_of(0, base + 4, first=True)
                    with pe.Fori(0, (FT - 4) // 2) as j:
                        for g in range(2, 4):
                            gate_up(g, base + 3 * g - 1, j * RING, j * 2)
                            down_of(g - 1, base + 3 * g + 1, j * RING, j * 2)
                    end = base + FFN_UNITS
                    gate_up(FT - 2, end - 7)
                    gate_up(FT - 1, end - 5)
                    down_of(FT - 3, end - 3)
                    down_last([hidden_of(FT - 2), hidden_of(FT - 1)], end - 2, [ready(FT - 2), ready(FT - 1)])

                def mixer():
                    base = MIX_BASE
                    pe.wait_ge(consts_ready, 2)
                    pre_and_first_units(1, base)
                    for q in range(2, NPAIR):
                        if q == 12:
                            pe.wait_ge(conv_in, layer + 1)
                        elif q == 13:
                            pe.wait_ge(mix_f, layer * 2 + 1)
                        else:
                            pe.wait_ge(z_evac, layer * 10 + q - 1)
                        name, _ = PAIRS[q]
                        if name == "av":
                            for t in range(TILES):
                                ins = token_major(Z[:, q % 2, t * SEQ:(t + 1) * SEQ], t, base + 2 * q, 2)
                            ins.then_inc(unit_used, 2)
                        else:
                            feature_major(Z[:, q % 2, 0:SEQ], base + 2 * q)
                            feature_major(Z[:, q % 2, SEQ:2 * SEQ], base + 2 * q + 1)
                        if q == FIRST_LEVEL_STEP + 1:
                            pe.wait_ge(z_evac, layer * 10 + 6)
                            pe.wait_ge(k_ready, layer + 1)
                            for i in range(8):
                                ins = pe.matmul(ACC[:, 2 + i // 4, i % 4 * P:(i % 4 + 1) * P],
                                                flat(K)[:, i * P:(i + 1) * P], flat(Q)[:, i * P:(i + 1) * P],
                                                start=True, stop=True)
                            ins.then_inc(own_ps, 1)
                        n = q - FIRST_LEVEL_STEP - 1
                        if 0 <= n <= NLV:
                            pe.wait_ge(level_in, layer * (NLV + 1) + n + 1)
                            if n >= 2:
                                pe.wait_ge(level_out, layer * (NLV + 1) + n - 1)
                            w = P // 2 if n < NLV else P
                            for i in range(HALF // w):
                                key = flat(KL)[:, i * P:(i + 1) * P] if n < NLV else KL[:, i, 0:P]
                                ins = pe.matmul(ACC[:, n % 2, i * w:(i + 1) * w], key, QL[:, i * w:(i + 1) * w],
                                                start=True, stop=True)
                            ins.then_inc(level_ps, 1)
                        if q == 8:
                            pe.wait_ge(z_evac, layer * 10 + 8)
                            pe.wait_ge(own_out, layer + 1)
                            for h in range(AT_HEADS):
                                pe.matmul(AUX[:, 0, h * P:(h + 1) * P], AQ[:, h // 2, 0:P], KZ[:, h, 0:P],
                                          start=True, stop=True)
                            for h in range(AT_HEADS):
                                ins = pe.matmul(ACC[:, 2 + h // 2, h % 2 * SEQ:(h % 2 + 1) * SEQ], AQ[:, h // 2, P:SEQ],
                                                KZ[:, h, :], start=True, stop=True)
                            ins.then_inc(qk_ps, 1)
                        if q == 10:
                            pe.wait_ge(pnorm, layer + 1)
                            for h in range(AT_HEADS):
                                pe.transpose(AUX[:, 0, h * P:(h + 1) * P], PA[:, h, :], ident[:, :])
                                for b in range(2):
                                    ins = pe.transpose(ACC[:, 2 + b, h * P:(h + 1) * P],
                                                       PB[:, h, b * P:(b + 1) * P], ident[:, :])
                            ins.then_inc(pT_ps, 1)
                        if q == 12:
                            pe.wait_ge(pT, layer * 2 + 2)
                            for h in range(AT_HEADS):
                                rows_ = slice(AT_DIM * (h % 2), AT_DIM * (h % 2) + AT_DIM)
                                to = AUX[rows_, 1, h // 2 * SEQ:(h // 2 + 1) * SEQ]
                                v = lambda b: AV[:, b, h * AT_DIM:(h + 1) * AT_DIM]
                                pe.matmul(to[:, 0:P], v(0), PTA[:, h, :], start=True, stop=True)
                                pe.matmul(to[:, P:SEQ], v(0), PTB[:, 0, h, :], start=True, stop=False)
                                ins = pe.matmul(to[:, P:SEQ], v(1), PTB[:, 1, h, :], start=False, stop=True)
                            ins.then_inc(at_ps, 1)
                    pe.wait_ge(level_out, layer * (NLV + 1) + NLV + 1)
                    pe.wait_ge(mix_lo, layer * 3 + 2)
                    pe.wait_ge(z_evac, layer * 10 + 9)
                    for h in range(HG_HEADS):
                        to = AUX[:, h // 2, h % 2 * SEQ:(h % 2 + 1) * SEQ]
                        v = lambda b: V[:, b, h * P:(h + 1) * P]
                        pe.matmul(to[:, 0:P], v(0), S[:, 2 * h, :], start=True, stop=True)
                        pe.matmul(to[:, P:SEQ], v(0), S10[:, h, :], start=True, stop=False)
                        ins = pe.matmul(to[:, P:SEQ], v(1), S[:, 2 * h + 1, :], start=False, stop=True)
                    ins.then_inc(o_ps, 1)
                    for o, kt in enumerate(OUT_ORDER):
                        if o == 2:
                            pe.wait_ge(o_sq, layer + 1)
                            pe.wait_ge(gate_done, layer * 2 + 2)
                            for a in range(2):
                                ins = pe.matmul(Z[:, a, :], ones[:, :], flat(D)[:, a * HALF:(a + 1) * HALF],
                                                start=True, stop=True)
                            ins.then_inc(ss_ps, 1)
                        if o % 2 == 0 and o <= 4:
                            pe.wait_ge(mix_lo, layer * 3 + o // 2 + 1)
                        if o < KT - 2:
                            down(mixT[:, :, kt, :], base + 2 * NPAIR + o, o == 0)
                    down_last([mixT[:, :, kt, :] for kt in OUT_ORDER[-2:]], base + 2 * NPAIR + KT - 2, None)

                ffn(0)
                mixer()
                ffn(1)



INPUTS = ["x", "norm_w", "ffn1_wg", "ffn1_wu", "ffn1_wd", "mix_w_in", "mix_w_out", "hg_lb", "hg_norm_w", "conv_w",
          "ffn2_wg", "ffn2_wu", "ffn2_wd", "rel_bias"]


def kernel(**inputs):
    import numpy as np
    import concourse.bacc as bacc
    from concourse.bass_utils import run_bass_kernel_spmd

    nc = bacc.Bacc("TRN2", target_bir_lowering=False, num_devices=1)
    f32 = mybir.dt.float32
    arrays = {f"in_{n}": np.ascontiguousarray(inputs[n]) for n in INPUTS}
    arrays["in_dist_onehot"] = np.array([[float(bucket(i - P) == b) for i in range(3 * P)]
                                         for b in range(BUCKETS)], np.float32)
    args = [nc.dram_tensor(n, a.shape, f32, kind="ExternalInput").ap() for n, a in arrays.items()]
    out = nc.dram_tensor("out_0", (1, SEQ, DM), f32, kind="ExternalOutput").ap()
    scratch = nc.dram_tensor("bias_scratch", (AT_HEADS, 3 * P), f32, kind="Internal").ap()
    trunk(nc, *args, out, scratch)
    r = run_bass_kernel_spmd(nc, [arrays], core_ids=[0])
    return r.results[0]["out_0"]
```

```python
from contextlib import ExitStack
import math

import concourse.bass as bass
from concourse import mybir

LAYERS, SEQ, DM, DFF = 2, 256, 1024, 2816
P = 128
TILES = SEQ // P
KT = DM // P
HG_HEADS, AT_HEADS, AT_DIM = 4, 4, 64
HG_WIDTH, AT_WIDTH, CV_WIDTH, TAPS = HG_HEADS * P, AT_HEADS * AT_DIM, 256, 3
BUCKETS, MAX_DIST = 32, 1024
EPS = 1e-6
NORMS = 6
SUB_FACTOR = (0.5, 1.0, 0.5)
FT = DFF // P
RING = 6
HALF = 512
FFN_UNITS = 3 * FT
W_IN_BLOCKS = {"hq": 0, "hf": 4, "hi": 8, "hg": 12, "aq": 16, "ak": 18, "av": 20, "cb": 22, "cc": 24, "ch": 26}
PAIRS = [("hi", 0), ("hi", 2), ("hf", 0), ("hf", 2), ("hq", 0), ("hq", 2), ("aq", 0), ("ak", 0), ("av", 0),
         ("cc", 0), ("ch", 0), ("cb", 0), ("hg", 0), ("hg", 2)]
OUT_ORDER = [6, 7, 4, 5, 0, 1, 2, 3]
NPAIR = len(PAIRS)
MIX_UNITS = 2 * NPAIR + KT
UNITS = 2 * FFN_UNITS + MIX_UNITS
FFN_BASE = [0, FFN_UNITS + MIX_UNITS]
MIX_BASE = FFN_UNITS
LEAD = 5
HELD = 3
LEVELS = [64, 32, 16, 8, 4, 2, 1]
NLV = len(LEVELS)
FIRST_LEVEL_STEP = 5
FROM = 2
MASKED = -1e30
ACT_STEPS, DVE_STEPS, POOL_STEPS = 15, 117, 12
E_MAX = 2.0 ** 60


def bucket(dist):
    dist = max(dist, 0)
    exact = BUCKETS // 2
    if dist < exact:
        return dist
    return min(BUCKETS - 1, exact + int(math.log(dist / exact) / math.log(MAX_DIST / exact) * (BUCKETS - exact)))


class Count:

    def __init__(self, semaphore, *rounds):
        self.semaphore, self.rounds, self.n, self.loops = semaphore, rounds, 0, []

    def enter(self, register):
        self.loops.append((register, self.n))

    def leave(self, times):
        each = self.rounds[len(self.loops) - 1]
        _, before = self.loops.pop()
        assert self.n - before == each, (self.n - before, each)
        self.n = before + each * times

    def done(self, instruction):
        instruction.then_inc(self.semaphore, 1)
        self.n += 1

    def wait(self, engine):
        value = self.n
        for (register, _), each in zip(self.loops, self.rounds):
            value = register * each + value
        engine.wait_ge(self.semaphore, value)


def trunk(nc, x_in, norm_w, f1_wg, f1_wu, f1_wd, w_in, w_out, hg_lb, hg_nw, conv_w,
          f2_wg, f2_wu, f2_wd, rel_bias, dist_onehot, out, bias_scratch):
    f32, f32r, u32, i32 = mybir.dt.float32, mybir.dt.float32r, mybir.dt.uint32, mybir.dt.int32
    ALU, ACT, AX = mybir.AluOpType, mybir.ActivationFunctionType, mybir.AxisListType
    ffn_w = [(f1_wg, f1_wu, f1_wd), (f2_wg, f2_wu, f2_wd)]

    with ExitStack() as ctx:
        def sb(name, shape, dt=f32):
            return ctx.enter_context(nc.sbuf_tensor(name, shape, dt))

        def sem(name):
            return ctx.enter_context(nc.semaphore(name))

        raw = sb("raw", [P, RING, DM])
        wsp = sb("wsp", [P, RING, 2, DM], f32r)
        x = sb("x", [P, TILES, DM])
        nw = sb("nw", [P, 3, DM])
        xT = sb("xT", [P, 2, KT, SEQ], f32r)
        hT = sb("hT", [P, 2, 2, SEQ], f32r)
        mixT = sb("mixT", [P, 2, KT, SEQ], f32r)

        ident = sb("ident", [P, P])
        ones = sb("ones", [P, P])
        level_mask = sb("level_mask", [P, NLV, P // 2])
        keep = sb("keep", [P, HG_HEADS * TILES, P])
        bias = sb("bias", [P, AT_HEADS, 2 * P])
        relb = sb("relb", [BUCKETS, AT_HEADS])
        onehot = sb("onehot", [BUCKETS, 3 * P])
        brow = sb("brow", [AT_HEADS, 3 * P])
        lb_raw = sb("lb_raw", [P, LAYERS, HG_HEADS])
        lb_all = sb("lb_all", [P, LAYERS, 2 * HG_HEADS])
        lb_tmp = sb("lb_tmp", [P, 8, HG_HEADS])
        cw_all = sb("cw_all", [P, LAYERS, TAPS * 2])
        nw_all = sb("nw_all", [P, LAYERS])
        lb = sb("lb", [P, 2 * HG_HEADS])
        cw = sb("cw", [P, TAPS * 2])
        hnw = sb("hnw", [P, 1])
        eps4 = sb("eps4", [P, 1])
        minus_half = sb("minus_half", [P, 1])
        st = sb("st", [P, TILES, 8])
        spare = sb("spare", [P, 4])

        Q = sb("Q", [P, HG_HEADS, SEQ])
        B = sb("B", [P, HG_HEADS, SEQ])
        K = sb("K", [P, HG_HEADS, SEQ])
        D = sb("D", [P, HG_HEADS, SEQ])
        KL = sb("KL", [P, HG_HEADS, SEQ])
        QL = sb("QL", [P, HALF])
        S = sb("S", [P, HG_HEADS * TILES, P])
        S10 = sb("S10", [P, HG_HEADS, P])
        V = sb("V", [P, TILES, HG_WIDTH])
        G = sb("G", [P, HG_HEADS, SEQ])
        AQ = sb("AQ", [P, 2, SEQ])
        KZ = sb("KZ", [P, AT_HEADS, SEQ])
        AV = sb("AV", [P, TILES, AT_WIDTH])
        PA = sb("PA", [P, AT_HEADS, P])
        PB = sb("PB", [P, AT_HEADS, SEQ])
        PTA = sb("PTA", [P, AT_HEADS, P])
        PTB = sb("PTB", [P, 2, AT_HEADS, P])
        C = sb("C", [P, 2, SEQ])
        U = sb("U", [P, 2, SEQ + 2])
        Y = sb("Y", [P, 2, SEQ])
        smax = sb("smax", [P, 8])
        snmax = sb("snmax", [P, 8])
        ssum = sb("ssum", [P, 8])
        srec = sb("srec", [P, 8])
        flat = lambda t: t[:, :, :].rearrange("p h t -> p (h t)")
        xn = [flat(D), flat(KL)]
        tmp = [flat(Q), flat(B)]
        junk = [flat(V), flat(G)]
        junk2 = [flat(PB), flat(K)]

        def level_exponents(engine, m, half):
            at = slice(half * HALF, (half + 1) * HALF)
            v = flat(B)[:, at].rearrange("p (g n) -> p g n", n=2 * m)
            return engine.tensor_tensor(flat(D)[:, at].rearrange("p (g n) -> p g n", n=2 * m), v,
                                        v[:, :, m - 1:m].broadcast_to([P, HALF // (2 * m), 2 * m]), ALU.subtract)

        hidden_of = lambda g: mixT[:, :, 0, :] if g == FT - 1 else hT[:, g % 2, :, :]
        ff = [flat(K)[:, 0:HALF], flat(K)[:, HALF:2 * HALF]]

        Z = ctx.enter_context(nc.psum_tensor("Z", [P, 2, HALF], f32))
        ACC = ctx.enter_context(nc.psum_tensor("ACC", [P, 4, HALF], f32))
        AUX = ctx.enter_context(nc.psum_tensor("AUX", [P, 2, HALF], f32))
        xpose_of = (AUX, ACC[:, 0:2, :])

        raw_loaded = [sem(f"raw_loaded{i}") for i in range(RING)]
        hi_done, split_done, unit_used = sem("hi_done"), sem("split_done"), sem("unit_used")
        lb_loaded, consts_loaded, onehot_loaded = sem("lb_loaded"), sem("consts_loaded"), sem("onehot_loaded")
        x_loaded = [sem(f"x_loaded{t}") for t in range(TILES)]
        nw_loaded = [sem(f"nw_loaded{i}") for i in range(3)]
        pool_chain, consts_ready, bias_ready = sem("pool_chain"), sem("consts_ready"), sem("bias_ready")
        brow_ps, brow_sb, scratch_written, hankel_loaded = (
            sem("brow_ps"), sem("brow_sb"), sem("scratch_written"), sem("hankel_loaded"))
        lb_shifted, lb_exp = sem("lb_shifted"), sem("lb_exp")
        x_squared, acc_squared, x_rms, acc_rms, scaled, xn_ready, xpose_done, xhi_done, xlo_done = (
            sem("x_squared"), sem("acc_squared"), sem("x_rms"), sem("acc_rms"), sem("scaled"), sem("xn_ready"),
            sem("xpose_done"), sem("xhi_done"), sem("xlo_done"))
        start_ps, acc_ready, x_done = sem("start_ps"), sem("acc_ready"), sem("x_done")
        tanh_ready, z_free, h_ready = sem("tanh_ready"), sem("z_free"), sem("h_ready")
        act_chain, dve_chain = sem("act_chain"), sem("dve_chain")
        z_evac, e_clamped, logs_ready = sem("z_evac"), sem("e_clamped"), sem("logs_ready")
        exponents, decays, level_in, level_ps, level_out, k_ready, own_ps, own_out, b_ready, pool_exponents = (
            sem("exponents"), sem("decays"), sem("level_in"), sem("level_ps"), sem("level_out"), sem("k_ready"),
            sem("own_ps"), sem("own_out"), sem("b_ready"), sem("pool_exponents"))
        qk_ps, logits, probs, pnorm, pT_ps, pT, at_ps = (
            sem("qk_ps"), sem("logits"), sem("probs"), sem("pnorm"), sem("pT_ps"), sem("pT"), sem("at_ps"))
        gate_tanh, gate_done, conv_in, mix_f, mix_hi, mix_lo = (
            sem("gate_tanh"), sem("gate_done"), sem("conv_in"), sem("mix_f"), sem("mix_hi"), sem("mix_lo"))
        o_ps, o_sq, ss_ps, o_rs, out_done = sem("o_ps"), sem("o_sq"), sem("ss_ps"), sem("o_rs"), sem("out_done")

        block = ctx.enter_context(nc.Block())

        @block.sync
        def _(sp):
            def load(layer, u, src, more=0, rounds=0, slots=1):
                if u < RING and rounds == 0:
                    sp.wait_ge(split_done, layer * (UNITS + u - RING + 1) + FROM)
                else:
                    if slots:
                        sp.wait_ge(split_done, layer * UNITS + more + (u - RING + slots) + FROM)
                sp.dma_start(raw[:, u % RING, :].rearrange("p (k n) -> p k n", n=src.shape[-1]), src)\
                  .then_inc(raw_loaded[u % RING], 16)

            def cols(w, layer, c):
                n = w.shape[2]
                return bass.AP(tensor=w.tensor, offset=sp.snap(layer * (w.shape[1] * n) + c),
                               ap=[[n, P], [P * n, KT], [1, P]])

            def rows(w, layer, r):
                n = w.shape[2]
                return bass.AP(tensor=w.tensor, offset=sp.snap(layer * (w.shape[1] * n) + r * n),
                               ap=[[n, P], [P * n, 1], [1, n]])

            sp.dma_start(onehot[:, :], dist_onehot).then_inc(onehot_loaded, 16)
            sp.dma_start(relb[:, :], rel_bias).then_inc(onehot_loaded, 16)
            with sp.Fori(0, LAYERS) as layer:
                def ffn(f):
                    wg, wu, wd = ffn_w[f]
                    base = FFN_BASE[f]
                    load(layer, base + 0, cols(wg, layer, 0))
                    load(layer, base + 1, cols(wu, layer, 0))
                    load(layer, base + 2, cols(wg, layer, P))
                    load(layer, base + 3, cols(wu, layer, P))
                    load(layer, base + 4, rows(wd, layer, 0))
                    with sp.Fori(0, (FT - 4) // 2) as j:
                        for i in range(2):
                            at = (base + 5 + 3 * i)
                            load(layer, at, cols(wg, layer, j * (2 * P) + (2 + i) * P), j * RING, 1)
                            load(layer, at + 1, cols(wu, layer, j * (2 * P) + (2 + i) * P), j * RING, 1)
                            load(layer, at + 2, rows(wd, layer, j * (2 * P) + (1 + i) * P), j * RING, 1)
                    for i, (w, first) in enumerate(((wg, FT - 2), (wu, FT - 2), (wg, FT - 1), (wu, FT - 1))):
                        load(layer, base + FFN_UNITS - 7 + i, cols(w, layer, first * P))
                    for i in (3, 2):
                        load(layer, base + FFN_UNITS - i, rows(wd, layer, DFF - i * P))
                    load(layer, base + FFN_UNITS - 1, rows(wd, layer, DFF - P))

                ffn(0)
                starts = [(W_IN_BLOCKS[name] + first + c) * P for name, first in PAIRS for c in range(2)]
                starts += [kt * P for kt in OUT_ORDER] + [None]
                for i, start in enumerate(starts[:-1]):
                    load(layer, MIX_BASE + i, cols(w_in, layer, start) if i < 2 * NPAIR else rows(w_out, layer, start),
                         slots=0 if start == 0 else 2 if starts[i + 1] == 0 else 1)
                ffn(1)
            for t in range(TILES):
                sp.wait_ge(x_done, LAYERS * NORMS - TILES + t + 1 + FROM)
                sp.dma_start(out[0, t * P:(t + 1) * P, :], x[:, t, :]).then_inc(out_done, 16)
            sp.wait_ge(out_done, 16 * TILES)

        @block.gpsimd
        def _(pool):
            chain = Count(pool_chain, POOL_STEPS)

            def link(ins):
                chain.done(ins)
                chain.wait(pool)

            def norm_load(i, layer):
                row = norm_w[bass.ds(layer, 1), i:i + 1, :].rearrange("a b n -> (a b) n")
                pool.dma_start(nw[:, i % 3, :], row.broadcast_to([P, DM])).then_inc(nw_loaded[i % 3], 16)

            def norm_used(i, layer):
                if i % 2:
                    pool.wait_ge(x_done, layer * 6 + 2 * (i // 2) + 2 + FROM)
                else:
                    pool.wait_ge(xn_ready, layer * 12 + 4 * (i // 2) + 4 + FROM)

            def inverse_rms_x(s, layer, t):
                pool.wait_ge(x_squared, layer * 6 + 2 * s + t + 1)
                v = st[:, t, 2:3]
                link(pool.tensor_scalar(v, st[:, t, 0:1], EPS, None, ALU.add))
                pool.tensor_tensor(st[:, t, 3:4], v, minus_half[:, :], ALU.pow).then_inc(x_rms, 1)

            def inverse_rms_acc(s, layer, t):
                pool.wait_ge(acc_squared, layer * 12 + 4 * s + 2 * t + 2)
                v = st[:, t, 6:7]
                link(pool.tensor_scalar(v, st[:, t, 4:5], st[:, t, 5:6], EPS / SUB_FACTOR[s] ** 2, ALU.add, ALU.add))
                pool.tensor_tensor(st[:, t, 7:8], v, minus_half[:, :], ALU.pow).then_inc(acc_rms, 1)

            link(pool.memset(ident[:, :], 0.0))
            link(pool.affine_select(out=ident[:, :], in_=ident[:, :], compare_op=ALU.not_equal, fill=1.0,
                                    base=0, pattern=[[-1, P]], channel_multiplier=1))
            link(pool.memset(minus_half[:, :], -0.5))
            pool.memset(eps4[:, :], 4 * EPS).then_inc(consts_ready, 1)
            norm_load(0, 0)
            for t in range(TILES):
                inverse_rms_x(0, 0, t)
            norm_load(1, 0)
            link(pool.memset(ones[:, :], 1.0))
            link(pool.memset(level_mask[:, :, :], 1.0))
            for n, m in enumerate(LEVELS):
                part = level_mask[:, n, :].rearrange("p (j m) -> p j m", m=m)
                link(pool.affine_select(out=part, in_=part, compare_op=ALU.is_ge, fill=0.0, base=0,
                                        pattern=[[-2 * m, P // (2 * m)], [0, m]], channel_multiplier=1))
                link(pool.affine_select(out=part, in_=part, compare_op=ALU.is_ge, fill=0.0, base=m - 1,
                                        pattern=[[2 * m, P // (2 * m)], [0, m]], channel_multiplier=-1))
            link(pool.memset(keep[:, :, :], 1.0))
            link(pool.memset(keep[:, :, 0:1], 0.0))
            link(pool.memset(KZ[:, :, :], 0.0))
            pool.memset(U[:, :, :], 0.0).then_inc(consts_ready, 1)
            pool.wait_ge(brow_sb, 1)
            pool.dma_start(bias_scratch, brow[:, :]).then_inc(scratch_written, 16)
            pool.wait_ge(scratch_written, 16)
            hankel = bass.AP(tensor=bias_scratch.tensor, offset=1, ap=[[1, P], [3 * P, AT_HEADS], [1, 2 * P]])
            rev = S[:, :, :].rearrange("p (h a) b -> p h (a b)", a=2)
            pool.dma_start(rev, hankel).then_inc(hankel_loaded, 16)
            pool.wait_ge(hankel_loaded, 16)
            link(pool.tensor_copy(bias[:, :, :], rev[:, :, ::-1]))
            pool.affine_select(out=bias[:, :, :], in_=bias[:, :, :], compare_op=ALU.is_ge, fill=MASKED, base=P,
                               pattern=[[0, AT_HEADS], [-1, 2 * P]], channel_multiplier=1).then_inc(bias_ready, 1)

            def norms(layer, following):
                for sub in range(3):
                    for i in (2 * sub - 1, 2 * sub):
                        if i + 3 < NORMS:
                            norm_used(i, layer)
                            norm_load(i + 3, layer)
                        elif following:
                            norm_used(i, layer)
                            norm_load(i + 3 - NORMS, layer + 1)
                    if sub == 1:
                        pool.wait_ge(b_ready, layer + 1)
                        for n, m in enumerate(LEVELS):
                            if n:
                                pool.wait_ge(level_in, layer * (NLV + 1) + n)
                            level_exponents(pool, m, 0).then_inc(pool_exponents, 1)
                    if sub == 0:
                        for t in range(TILES):
                            inverse_rms_acc(0, layer, t)
                            inverse_rms_x(1, layer, t)
                    else:
                        for t in range(TILES):
                            inverse_rms_acc(sub, layer, t)
                        for t in range(TILES):
                            if sub == 1:
                                inverse_rms_x(2, layer, t)
                            elif following:
                                inverse_rms_x(0, layer + 1, t)

            with pool.Fori(0, LAYERS - 1) as layer:
                chain.enter(layer)
                norms(layer, True)
                chain.leave(LAYERS - 1)
            norms(LAYERS - 1, False)
            for i in range(3):
                pool.wait_ge(nw_loaded[i], 16 * 2 * LAYERS)

        @block.scalar
        def _(act):
            chain = Count(act_chain, ACT_STEPS)

            act.dma_start(lb_raw[:, :, :], hg_lb.rearrange("l (h p) -> p l h", p=P),
                          allow_slow_non_contiguous=True).then_inc(lb_loaded, 16)
            for t in range(TILES):
                act.dma_start(x[:, t, :], x_in[0, t * P:(t + 1) * P, :]).then_inc(x_loaded[t], 16)
            act.dma_start(cw_all[:, :, :].rearrange("p l (w c) -> p (l w) c", c=2),
                          conv_w.rearrange("l w (c p) -> p (l w) c", p=P), allow_slow_non_contiguous=True)\
               .then_inc(consts_loaded, 16)
            act.dma_start(nw_all[:, :], hg_nw.rearrange("l p -> p l"), allow_slow_non_contiguous=True)\
               .then_inc(consts_loaded, 16)

            act.wait_ge(lb_shifted, 1)
            act.activation(lb_tmp[:, 1:3, :], lb_tmp[:, 1:3, :], ACT.Exp).then_inc(lb_exp, 1)
            act.wait_ge(consts_ready, 1)

            with act.Fori(0, LAYERS) as layer:
                chain.enter(layer)

                def U_(u, more=0):
                    return layer * UNITS + more + u

                def split(u, more=0, rounds=0):
                    act.wait_ge(raw_loaded[u % RING], (layer * (UNITS // RING) + rounds + (u // RING + 1)) * 16)
                    act.wait_ge(unit_used, (layer * UNITS if u < RING else U_(u - RING + 1, more)) + FROM)
                    act.activation(wsp[:, u % RING, 0, :], raw[:, u % RING, :], ACT.Copy).then_inc(hi_done, 1)

                def squares_x(s, t):
                    act.wait_ge(x_done, layer * NORMS + 2 * s + t - 1 + FROM)
                    if s == 0:
                        act.wait_ge(x_loaded[t], 16)
                    act.activation(junk[t], x[:, t, :], ACT.Square, scale=DM ** -0.5, accum_out=st[:, t, 0:1])\
                       .then_inc(x_squared, 1)

                def squares_acc(s, t, h):
                    if h:
                        act.wait_ge(scaled, layer * 12 + 4 * s + 2 * t + 1)
                    elif t == 0:
                        act.wait_ge(acc_ready, layer * 3 + s + 1)
                    else:
                        act.wait_ge(unit_used, U_((FFN_UNITS, FFN_BASE[1], UNITS)[s]) + FROM)
                    act.activation(junk2[t][:, h * HALF:(h + 1) * HALF], ACC[:, 2 * t + h, :], ACT.Square,
                                   scale=DM ** -0.5 / SUB_FACTOR[s], accum_out=st[:, t, 4 + h:5 + h])\
                       .then_inc(acc_squared, 1)

                def high(s, t):
                    for h in range(2):
                        act.wait_ge(xpose_done, layer * 12 + 4 * s + 2 * t + h + 1)
                        act.activation(xT[:, 0, 4 * h:4 * h + 4, t * P:(t + 1) * P],
                                       xpose_of[t][:, h, :].rearrange("p (k n) -> p k n", k=4), ACT.Copy)\
                           .then_inc(xhi_done, 1)

                def layer_start():
                    split(0)
                    for t in range(TILES):
                        squares_x(0, t)
                    for t in range(TILES):
                        high(0, t)
                    for u in range(1, LEAD):
                        split(u)

                def between(s):
                    following = (MIX_BASE, FFN_BASE[1], None)[s]
                    squares_acc(s, 0, 0)
                    squares_acc(s, 0, 1)
                    if s == 0:
                        split(following + RING - HELD)
                        squares_x(1, 0)
                    squares_acc(s, 1, 0)
                    squares_acc(s, 1, 1)
                    if s == 0:
                        high(1, 0)
                        split(following + LEAD - 1)
                        squares_x(1, 1)
                        high(1, 1)
                    elif s == 1:
                        squares_x(2, 0)
                        squares_x(2, 1)
                        high(2, 0)
                        high(2, 1)
                        for u in range(RING - HELD, LEAD):
                            split(following + u)

                def ffn(f):
                    base = FFN_BASE[f]

                    def gate(g, more=0):
                        used = 2 if g == 0 else 3 * g if g == FT - 1 else 3 * g + 1
                        act.wait_ge(unit_used, U_(base + used, more) + FROM)
                        act.activation(ff[g % 2][:, 0:SEQ], Z[:, g % 2, 0:SEQ], ACT.Tanh, scale=0.5)\
                           .then_inc(tanh_ready, 1)

                    for g in range(2):
                        gate(g)
                        for i in range(3):
                            split(base + LEAD + 3 * g + i)
                    with act.Fori(0, (FT - 4) // 2) as j:
                        for g in range(2, 4):
                            gate(g, j * RING)
                            for i in range(3):
                                split(base + LEAD + 3 * g + i, j * RING, j)
                    last = FT - 2
                    gate(last)
                    split(base + FFN_UNITS - 1)
                    if f == 0:
                        split(base + FFN_UNITS)
                    gate(last + 1)
                    if f == 0:
                        for i in range(1, RING - HELD):
                            split(base + FFN_UNITS + i)

                def mixer():
                    base = MIX_BASE

                    def evac(dst, src):
                        act.activation(dst, src, ACT.Copy).then_inc(z_evac, 1)

                    for q in range(NPAIR + KT // 2):
                        if q < NPAIR + KT // 2 - 1:
                            split(base + LEAD + 2 * q)
                        if q == 12:
                            act.wait_ge(pT_ps, layer + 1)
                            act.activation(PTA[:, :, :], AUX[:, 0, :].rearrange("p (h t) -> p h t", h=4), ACT.Copy)\
                               .then_inc(pT, 1)
                            act.activation(PTB[:, :, :, :].rearrange("p a h t -> p a (h t)"), ACC[:, 2:4, :], ACT.Copy)\
                               .then_inc(pT, 1)
                        if q == 13:
                            act.wait_ge(at_ps, layer + 1)
                            act.activation(mixT[:, 0, 4:6, :], AUX[:, 1, :].rearrange("p (a t) -> p a t", a=2),
                                           ACT.Copy).then_inc(mix_hi, 1)
                        if q < NPAIR:
                            if q == 0:
                                act.wait_ge(start_ps, layer + 1)
                            else:
                                act.wait_ge(unit_used, U_(base + 2 * q + 2) + FROM)
                            z = Z[:, q % 2, :]
                            name, first = PAIRS[q]
                            two = z.rearrange("p (h t) -> p h t", h=2)
                            if name == "hf":
                                act.activation(K[:, first:first + 2, :], two, ACT.Exp, scale=-1.0).then_inc(z_evac, 1)
                            elif name == "hq":
                                evac(Q[:, first:first + 2, :], two)
                            elif name == "aq":
                                evac(AQ[:, :, :], two)
                            elif name == "ak":
                                chain.done(act.activation(KZ[0:AT_DIM, 0:4:2, :], two[0:AT_DIM, :, :], ACT.Copy))
                                evac(KZ[AT_DIM:P, 1:4:2, :], two[AT_DIM:P, :, :])
                            elif name == "av":
                                evac(AV[:, :, :], two)
                            elif name == "hi":
                                evac(V[:, q, :], z)
                            elif name == "hg":
                                act.activation(G[:, first:first + 2, :], two, ACT.Tanh, scale=0.5)\
                                   .then_inc(gate_tanh, 1)
                            elif name == "cc":
                                evac(C[:, :, :], two)
                        if q == 3:
                            split(base + LEAD + 2 * q + 1)
                            act.wait_ge(e_clamped, layer + 1)
                            chain.done(act.activation(flat(D), flat(K), ACT.Ln, bias=1.0))
                            for h in range(HG_HEADS):
                                chain.done(act.activation(B[:, h, :], K[:, h, :], ACT.Ln, bias=1.0,
                                                          scale=lb[:, h:h + 1]))
                            chain.wait(act)
                            act.activation(flat(KL), flat(D), ACT.Exp, scale=-1.0).then_inc(logs_ready, 1)
                        n = q - FIRST_LEVEL_STEP
                        if 0 <= n <= NLV:
                            act.wait_ge(exponents, layer * (NLV + 1) + n + 1)
                            if n < NLV:
                                act.wait_ge(pool_exponents, layer * NLV + n + 1)
                            if n < NLV:
                                v = flat(D).rearrange("p (g q m) -> p g q m", q=2, m=LEVELS[n])
                                chain.done(act.activation(v[:, :, 0, :], v[:, :, 0, :], ACT.Exp, scale=-1.0))
                                act.activation(v[:, :, 1, :], v[:, :, 1, :], ACT.Exp).then_inc(decays, 1)
                            else:
                                chain.done(act.activation(D[:, :, 0:P], D[:, :, 0:P], ACT.Exp, scale=-1.0))
                                act.activation(D[:, :, P:SEQ], B[:, :, P:SEQ], ACT.Exp).then_inc(decays, 1)
                        if q != 3 and q < NPAIR + KT // 2 - 1:
                            split(base + LEAD + 2 * q + 1)
                        if q == 8:
                            act.wait_ge(logits, layer + 1)
                            for h in range(AT_HEADS):
                                act.activation(PA[:, h, :], PA[:, h, :], ACT.Exp, bias=snmax[:, h:h + 1],
                                               accum_out=ssum[:, h:h + 1]).then_inc(probs, 1)
                                act.activation(PB[:, h, :], PB[:, h, :], ACT.Exp, bias=snmax[:, 4 + h:5 + h],
                                               accum_out=ssum[:, 4 + h:5 + h]).then_inc(probs, 1)
                        if q == 12:
                            act.wait_ge(mix_f, layer * 2 + 1)
                            act.activation(mixT[:, 0, 6:8, :], Y[:, :, :], ACT.Copy).then_inc(mix_hi, 1)
                        if q == NPAIR - 1:
                            act.wait_ge(o_ps, layer + 1)
                            act.activation(flat(D), AUX[:, :, :].rearrange("p a b -> p (a b)"), ACT.Square)\
                               .then_inc(o_sq, 1)
                        if q == NPAIR:
                            act.wait_ge(ss_ps, layer + 1)
                            chain.done(act.activation(flat(K), Z[:, :, :].rearrange("p a b -> p (a b)"), ACT.Ln,
                                                      bias=eps4[:, :], scale=4.0 / P))
                            chain.wait(act)
                            act.activation(flat(K), flat(K), ACT.Exp, scale=-0.5).then_inc(o_rs, 1)
                            act.wait_ge(mix_f, layer * 2 + 2)
                            act.activation(mixT[:, 0, 0:4, :], Q[:, :, :], ACT.Copy).then_inc(mix_hi, 1)

                layer_start()
                ffn(0)
                between(0)
                mixer()
                between(1)
                ffn(1)
                between(2)
                chain.leave(LAYERS)

        @block.vector
        def _(dve):
            chain = Count(dve_chain, DVE_STEPS, 4)

            def link(ins):
                chain.done(ins)
                chain.wait(dve)

            for i, started in enumerate((split_done, xn_ready, x_done)):
                dve.memset(spare[:, i:i + 1], 0.0).then_inc(started, FROM)
            dve.wait_ge(lb_loaded, 16)
            a = [lb_raw[:, l, :] for l in range(LAYERS)]
            mx, e0, e1, tot, rec, s0, s1, cum = [lb_tmp[:, i, :] for i in range(8)]
            link(dve.tensor_tensor(mx, a[0], a[1], ALU.max))
            link(dve.tensor_tensor(e0, a[0], mx, ALU.subtract))
            dve.tensor_tensor(e1, a[1], mx, ALU.subtract).then_inc(lb_shifted, 1)
            dve.wait_ge(lb_exp, 1)
            link(dve.tensor_tensor(tot, e0, e1, ALU.add))
            link(dve.reciprocal(rec, tot))
            link(dve.tensor_tensor(s0, e0, rec, ALU.mult))
            link(dve.tensor_tensor(s1, e1, rec, ALU.mult))
            link(dve.tensor_tensor(cum, s0, s1, ALU.add))
            link(dve.tensor_tensor(lb_all[:, 0, 0:HG_HEADS], s0, s0, ALU.subtract))
            link(dve.tensor_tensor(lb_all[:, 1, 0:HG_HEADS], cum, s0, ALU.subtract))
            link(dve.tensor_scalar(lb_all[:, :, HG_HEADS:], lb_all[:, :, 0:HG_HEADS], -1.0, 1.0, ALU.mult, ALU.add))
            dve.wait_ge(brow_ps, 1)
            dve.tensor_copy(brow[:, :], AUX[0:AT_HEADS, 0, 0:3 * P]).then_inc(brow_sb, 1)

            with dve.Fori(0, LAYERS) as layer:
                chain.enter(layer)

                def U_(u, more=0):
                    return layer * UNITS + more + u

                def split(u, more=0):
                    dve.wait_ge(hi_done, U_(u + 1, more))
                    dve.tensor_tensor(wsp[:, u % RING, 1, :], raw[:, u % RING, :],
                                      wsp[:, u % RING, 0, :].bitcast(f32), ALU.subtract).then_inc(split_done, 1)

                def weights_of(i):
                    dve.wait_ge(nw_loaded[i % 3], (layer * 2 + (i // 3 + 1)) * 16)
                    return nw[:, i % 3, :]

                def normed(s, t):
                    w = weights_of(2 * s)
                    dve.wait_ge(x_rms, layer * 6 + 2 * s + t + 1)
                    for h in range(2):
                        half = slice(h * HALF, (h + 1) * HALF)
                        dve.scalar_tensor_tensor(xn[t][:, half], x[:, t, half], st[:, t, 3:4], w[:, half],
                                                 ALU.mult, ALU.mult).then_inc(xn_ready, 1)

                def low(s, t):
                    at = slice(t * P, (t + 1) * P)
                    for h in range(2):
                        dve.wait_ge(xhi_done, layer * 12 + 4 * s + 2 * t + h + 1)
                        dve.tensor_tensor(xT[:, 1, 4 * h:4 * h + 4, at],
                                          xpose_of[t][:, h, :].rearrange("p (k n) -> p k n", k=4),
                                          xT[:, 0, 4 * h:4 * h + 4, at].bitcast(f32), ALU.subtract)\
                           .then_inc(xlo_done, 1)

                def layer_start():
                    split(0)
                    for t in range(TILES):
                        normed(0, t)
                    for t in range(TILES):
                        low(0, t)
                    for u in range(1, LEAD):
                        split(u)

                def between(s):
                    following = (MIX_BASE, FFN_BASE[1], None)[s]
                    w = weights_of(2 * s + 1)

                    def scale(t):
                        if t == 0:
                            dve.wait_ge(acc_ready, layer * 3 + s + 1)
                        else:
                            dve.wait_ge(unit_used, U_((FFN_UNITS, FFN_BASE[1], UNITS)[s]) + FROM)
                        for h in (1, 0):
                            if h == 0:
                                dve.wait_ge(acc_squared, layer * 12 + 4 * s + 2 * t + 1)
                            half = slice(h * HALF, (h + 1) * HALF)
                            dve.tensor_tensor(tmp[t][:, half], ACC[:, 2 * t + h, :], w[:, half], ALU.mult)\
                               .then_inc(scaled, 1)

                    def add(t):
                        dve.wait_ge(scaled, layer * 12 + 4 * s + 2 * t + 2)
                        dve.wait_ge(acc_rms, layer * 6 + 2 * s + t + 1)
                        dve.scalar_tensor_tensor(x[:, t, :], tmp[t], st[:, t, 7:8], x[:, t, :], ALU.mult, ALU.add)\
                           .then_inc(x_done, 1)

                    scale(0)
                    add(0)
                    if s == 0:
                        split(following + RING - HELD)
                    scale(1)
                    if s == 0:
                        normed(1, 0)
                    add(1)
                    if s == 0:
                        low(1, 0)
                        split(following + LEAD - 1)
                        normed(1, 1)
                        low(1, 1)
                    elif s == 1:
                        normed(2, 0)
                        normed(2, 1)
                        low(2, 0)
                        low(2, 1)
                        for u in range(RING - HELD, LEAD):
                            split(following + u)

                def ffn(f):
                    base = FFN_BASE[f]

                    def hidden(g, more=0, rounds=0):
                        dve.wait_ge(tanh_ready, layer * (2 * FT) + rounds + (FT * f + g + 1))
                        e, h = ff[g % 2][:, 0:SEQ], ff[g % 2][:, SEQ:2 * SEQ]
                        link(dve.scalar_tensor_tensor(e, e, 1.0, Z[:, g % 2, 0:SEQ], ALU.add, ALU.mult))
                        link(dve.scalar_tensor_tensor(h, e, 0.5, Z[:, g % 2, SEQ:2 * SEQ], ALU.mult, ALU.mult))
                        to = hidden_of(g)
                        if 2 <= g < FT - 1:
                            dve.wait_ge(unit_used, U_(base + 4 + 3 * (g - 2) + 1, more) + FROM)
                        dve.tensor_copy(to[:, 0, :], h).then_inc(z_free, 1)
                        dve.wait_ge(z_free, layer * (2 * FT) + rounds + (FT * f + g + 1))
                        dve.tensor_tensor(to[:, 1, :], h, to[:, 0, :].bitcast(f32), ALU.subtract)\
                           .then_inc(h_ready, 1)

                    for g in range(2):
                        hidden(g)
                        for i in range(3):
                            split(base + LEAD + 3 * g + i)
                    with dve.Fori(0, (FT - 4) // 2) as j:
                        chain.enter(j)
                        for g in range(2, 4):
                            hidden(g, j * RING, j * 2)
                            for i in range(3):
                                split(base + LEAD + 3 * g + i, j * RING)
                        chain.leave((FT - 4) // 2)
                    last = FT - 2
                    hidden(last)
                    split(base + FFN_UNITS - 1)
                    if f == 0:
                        split(base + FFN_UNITS)
                    hidden(last + 1)
                    if f == 0:
                        for i in range(1, RING - HELD):
                            split(base + FFN_UNITS + i)

                def mixer():
                    base = MIX_BASE
                    z_of = lambda q: Z[:, q % 2, :].rearrange("p (h t) -> p h t", h=2)
                    dve.wait_ge(consts_ready, 2)
                    dve.wait_ge(consts_loaded, 32)
                    chain.done(dve.tensor_copy(lb[:, :], lb_all[:, bass.ds(layer, 1), :].rearrange("p a n -> p (a n)")))
                    chain.done(dve.tensor_copy(cw[:, :], cw_all[:, bass.ds(layer, 1), :].rearrange("p a n -> p (a n)")))
                    link(dve.tensor_copy(hnw[:, :], nw_all[:, bass.ds(layer, 1)]))
                    dve.wait_ge(bias_ready, 1)
                    link(dve.memset(S[:, :, :], 0.0))
                    for q in range(NPAIR + KT // 2):
                        if q == 3:
                            dve.wait_ge(z_evac, layer * 10 + 4)
                            dve.tensor_scalar(flat(K), flat(K), E_MAX, None, ALU.min).then_inc(e_clamped, 1)
                        if q == 4:
                            dve.wait_ge(logs_ready, layer + 1)
                            chain.done(dve.tensor_tensor(flat(B), flat(B), flat(D), ALU.subtract))
                            for h in range(HG_HEADS):
                                ins = dve.scalar_tensor_tensor(K[:, h, :], K[:, h, :], lb[:, HG_HEADS + h:HG_HEADS + h + 1],
                                                               KL[:, h, :], ALU.mult, ALU.mult)
                                if h < HG_HEADS - 1:
                                    chain.done(ins)
                            ins.then_inc(k_ready, 1)
                            chain.wait(dve)
                            dve.tensor_tensor_scan(flat(B), keep[:, :, :].rearrange("p g t -> p (g t)"), flat(B),
                                                   0.0, ALU.mult, ALU.add).then_inc(b_ready, 1)
                            dve.wait_ge(b_ready, layer + 1)
                        n = q - FIRST_LEVEL_STEP
                        if 1 <= n <= NLV:
                            dve.wait_ge(level_in, layer * (NLV + 1) + n)
                        if 0 <= n < NLV:
                            m = LEVELS[n]
                            level_exponents(dve, m, 1).then_inc(exponents, 1)
                        if n == NLV:
                            dve.tensor_tensor(D[:, :, 0:P], B[:, :, 0:P],
                                              B[:, :, P - 1:P].broadcast_to([P, HG_HEADS, P]), ALU.subtract)\
                               .then_inc(exponents, 1)
                        if q == NPAIR + 1:
                            dve.wait_ge(mix_hi, layer * 3 + 3)
                            dve.tensor_tensor(mixT[:, 1, 0:4, :], Q[:, :, :], mixT[:, 0, 0:4, :].bitcast(f32),
                                              ALU.subtract).then_inc(mix_lo, 1)
                        if q < NPAIR + KT // 2 - 1:
                            split(base + LEAD + 2 * q)
                        if q == 13:
                            dve.wait_ge(mix_hi, layer * 3 + 1)
                            dve.tensor_tensor(mixT[:, 1, 6:8, :], Y[:, :, :], mixT[:, 0, 6:8, :].bitcast(f32),
                                              ALU.subtract).then_inc(mix_lo, 1)
                            dve.wait_ge(mix_hi, layer * 3 + 2)
                            dve.tensor_tensor(mixT[:, 1, 4:6, :], AUX[:, 1, :].rearrange("p (a t) -> p a t", a=2),
                                              mixT[:, 0, 4:6, :].bitcast(f32), ALU.subtract).then_inc(mix_lo, 1)
                        if q < 5:
                            split(base + LEAD + 2 * q + 1)
                        if 0 <= n <= NLV:
                            dve.wait_ge(decays, layer * (NLV + 1) + n + 1)
                            dve.wait_ge(z_evac, layer * 10 + 6)
                            if n:
                                dve.wait_ge(level_ps, layer * (NLV + 1) + n)
                            if n < NLV:
                                by = lambda t: flat(t).rearrange("p (g q m) -> p g q m", q=2, m=LEVELS[n])
                                chain.done(dve.tensor_tensor(by(KL)[:, :, 0, :], by(K)[:, :, 0, :], by(D)[:, :, 0, :],
                                                             ALU.mult))
                                dve.tensor_tensor(QL[:, :].rearrange("p (g m) -> p g m", m=LEVELS[n]),
                                                  by(Q)[:, :, 1, :], by(D)[:, :, 1, :], ALU.mult).then_inc(level_in, 1)
                            else:
                                chain.done(dve.tensor_tensor(KL[:, :, 0:P], K[:, :, 0:P], D[:, :, 0:P], ALU.mult))
                                dve.tensor_tensor(QL[:, :].rearrange("p (g m) -> p g m", m=P),
                                                  Q[:, :, P:SEQ], D[:, :, P:SEQ], ALU.mult).then_inc(level_in, 1)
                        if 5 <= q < NPAIR - 1:
                            split(base + LEAD + 2 * q + 1)
                        if q == FIRST_LEVEL_STEP + 1:
                            dve.wait_ge(own_ps, layer + 1)
                            mask = ident[:, :].bitcast(u32).rearrange("p (g t) -> p g t", g=1).broadcast_to([P, 8, P])
                            dve.memset(spare[:, 3:4], 0.0)
                            dve.copy_predicated(S[:, :, :], mask, ACC[:, 2:4, :].rearrange(
                                "p a (g t) -> p (a g) t", t=P)).then_inc(own_out, 1)
                            dve.wait_ge(own_out, layer + 1)
                        c = n - 1
                        if 0 <= c <= NLV:
                            dve.wait_ge(level_ps, layer * (NLV + 1) + c + 1)
                            if c:
                                dve.wait_ge(level_out, layer * (NLV + 1) + c)
                            if c < NLV:
                                m = LEVELS[c]
                                into = S[:, :, :].rearrange("p g (j q m) -> p g j q m", q=2, m=m)[:, :, :, 1, :]
                                mask = level_mask[:, c, :].bitcast(u32).rearrange("p (g j m) -> p g j m", g=1, m=m)\
                                    .broadcast_to([P, 8, P // (2 * m), m])
                                dve.memset(spare[:, 3:4], 0.0)
                                dve.copy_predicated(into, mask, ACC[:, c % 2, :].rearrange(
                                    "p (g j m) -> p g j m", g=8, m=m)).then_inc(level_out, 1)
                            else:
                                dve.tensor_copy(S10[:, :, :], ACC[:, NLV % 2, :].rearrange("p (h t) -> p h t", h=4))\
                                   .then_inc(level_out, 1)
                        if NPAIR - 1 <= q < NPAIR + KT // 2 - 1:
                            split(base + LEAD + 2 * q + 1)
                        if q == 8:
                            dve.wait_ge(qk_ps, layer + 1)
                            scale = float(AT_DIM) ** -0.5
                            chain.done(dve.scalar_tensor_tensor(
                                PA[:, :, :], AUX[:, 0, :].rearrange("p (h t) -> p h t", h=4), scale,
                                bias[:, :, P:2 * P], ALU.mult, ALU.add))
                            link(dve.scalar_tensor_tensor(
                                PB[:, :, :], ACC[:, 2:4, :].rearrange("p a (h t) -> p (a h) t", t=SEQ), scale,
                                bias[:, :, :], ALU.mult, ALU.add))
                            chain.done(dve.reduce_max(smax[:, 0:4], PA[:, :, :], AX.X))
                            link(dve.reduce_max(smax[:, 4:8], PB[:, :, :], AX.X))
                            dve.tensor_scalar(snmax[:, :], smax[:, :], -1.0, None, ALU.mult).then_inc(logits, 1)
                        if q == 9:
                            dve.wait_ge(probs, layer * 8 + 8)
                            link(dve.reciprocal(srec[:, :], ssum[:, :]))
                            chain.done(dve.tensor_tensor(PA[:, :, :], PA[:, :, :], srec[:, 0:4].rearrange(
                                "p (h a) -> p h a", a=1).broadcast_to([P, 4, P]), ALU.mult))
                            dve.tensor_tensor(PB[:, :, :], PB[:, :, :], srec[:, 4:8].rearrange(
                                "p (h a) -> p h a", a=1).broadcast_to([P, 4, SEQ]), ALU.mult).then_inc(pnorm, 1)
                        if q < NPAIR and PAIRS[q][0] == "hg":
                            first = PAIRS[q][1]
                            part = G[:, first:first + 2, :]
                            dve.wait_ge(gate_tanh, layer * 2 + first // 2 + 1)
                            dve.scalar_tensor_tensor(part, part, 1.0, z_of(q), ALU.add, ALU.mult).then_inc(gate_done, 1)
                        if q == 10:
                            dve.wait_ge(z_evac, layer * 10 + 10)
                            dve.wait_ge(unit_used, U_(base + 2 * q + 2) + FROM)
                            dve.tensor_tensor(U[:, :, 2:], z_of(q), C[:, :, :], ALU.mult).then_inc(conv_in, 1)
                            dve.wait_ge(conv_in, layer + 1)
                            tap = lambda i, c_: cw[:, 2 * i + c_:2 * i + c_ + 1]
                            for c_ in range(2):
                                chain.done(dve.tensor_scalar(Y[:, c_, :], U[:, c_, 2:], tap(2, c_), None, ALU.mult))
                            for i in (1, 0):
                                chain.wait(dve)
                                for c_ in range(2):
                                    chain.done(dve.scalar_tensor_tensor(Y[:, c_, :], U[:, c_, i:i + SEQ], tap(i, c_),
                                                                        Y[:, c_, :], ALU.mult, ALU.add))
                            chain.wait(dve)
                        if q == 11:
                            dve.wait_ge(unit_used, U_(base + 2 * q + 2) + FROM)
                            dve.tensor_tensor(Y[:, :, :], z_of(q), Y[:, :, :], ALU.mult).then_inc(mix_f, 1)
                        if q == NPAIR - 1:
                            dve.wait_ge(gate_done, layer * 2 + 2)
                            dve.wait_ge(o_sq, layer + 1)
                            link(dve.scalar_tensor_tensor(flat(Q), AUX[:, :, :].rearrange("p a b -> p (a b)"),
                                                          hnw[:, :], flat(G), ALU.mult, ALU.mult))
                        if q == NPAIR + 1 - 1:
                            dve.wait_ge(o_rs, layer + 1)
                            dve.tensor_tensor(flat(Q), flat(Q), flat(K), ALU.mult).then_inc(mix_f, 1)

                layer_start()
                ffn(0)
                between(0)
                mixer()
                between(1)
                ffn(1)
                between(2)
                chain.leave(LAYERS)

        @block.tensor
        def _(pe):
            pe.wait_ge(onehot_loaded, 32)
            pe.matmul(AUX[0:AT_HEADS, 0, 0:P], relb[:, :], onehot[:, 0:P], start=True, stop=True)\
              .then_inc(unit_used, FROM)
            pe.matmul(AUX[0:AT_HEADS, 0, P:3 * P], relb[:, :], onehot[:, P:3 * P], start=True, stop=True)\
              .then_inc(brow_ps, 1)
            pe.wait_ge(consts_ready, 1)

            PRODUCTS = ((0, 0), (0, 1), (1, 0))

            with pe.Fori(0, LAYERS) as layer:
                def U_(u, more=0):
                    return layer * UNITS + more + u

                def contract(product, arrived=None, parts=(0, 1)):
                    for b in parts:
                        for k in range(KT):
                            if arrived and k % (KT // 2) == 0:
                                arrived(b, k // (KT // 2))
                            for a in (0, 1)[:2 - b]:
                                ins = product(a, b, k, k == 0 and a + b == 0, k == KT - 1 and b == 1)
                    return ins

                def arrived(s, t):
                    def wait(b, h):
                        pe.wait_ge((xhi_done, xlo_done)[b], layer * 12 + 4 * s + 2 * t + h + 1)
                    return wait

                def feature_major(dst, u, more=0, arrived=None):
                    pe.wait_ge(split_done, U_(u + 1, more) + FROM)
                    contract(lambda a, b, k, start, stop: pe.matmul(
                        dst, wsp[:, u % RING, a, k * P:(k + 1) * P], xT[:, b, k, :], start=start, stop=stop),
                        arrived).then_inc(unit_used, 1)

                def token_major(dst, t, u, units, arrived=None, parts=(0, 1)):
                    pe.wait_ge(split_done, U_(u + units) + FROM)
                    s = u % RING
                    return contract(lambda a, b, k, start, stop: pe.matmul(
                        dst.rearrange("p (c n) -> p c n", c=units), xT[:, b, k, t * P:(t + 1) * P],
                        wsp[:, s:s + units, a, k * P:(k + 1) * P], start=start, stop=stop), arrived, parts)

                def down_tile(left, u, t, first, last, more=0):
                    for a, b in PRODUCTS:
                        for h in range(2):
                            ins = pe.matmul(ACC[:, 2 * t + h, :], left[:, b, t * P:(t + 1) * P],
                                            wsp[:, u % RING, a, h * HALF:(h + 1) * HALF],
                                            start=(first and a + b == 0), stop=(last and a == 1))
                    return ins

                def down(left, u, first, more=0):
                    pe.wait_ge(split_done, U_(u + 1, more) + FROM)
                    down_tile(left, u, 0, first, False)
                    down_tile(left, u, 1, first, False).then_inc(unit_used, 1)

                def down_last(lefts, u, ready=None):
                    for i in range(HELD):
                        pe.wait_ge(split_done, U_(u + i + 1) + FROM)
                        if ready:
                            pe.wait_ge(*ready[i])
                        ins = down_tile(lefts[i], u + i, 0, False, i == HELD - 1)
                    ins.then_inc(acc_ready, 1)
                    for i in range(HELD):
                        down_tile(lefts[i], u + i, 1, False, i == HELD - 1).then_inc(unit_used, 1)

                def transposes(s, t):
                    for h in range(2):
                        pe.wait_ge(xn_ready, layer * 12 + 4 * s + 2 * t + h + 1 + FROM)
                        for k in range(4):
                            ins = pe.transpose(xpose_of[t][:, h, k * P:(k + 1) * P],
                                               xn[t][:, (4 * h + k) * P:(4 * h + k + 1) * P], ident[:, :])
                        ins.then_inc(xpose_done, 1)

                def pre_and_first_units(s, u):
                    transposes(s, 0)
                    token_major(Z[:, 0, :], 0, u, 4, arrived(s, 0), parts=(0,))
                    transposes(s, 1)
                    token_major(Z[:, 0, :], 0, u, 4, arrived(s, 0), parts=(1,)).then_inc(start_ps, 1)
                    token_major(Z[:, 1, :], 1, u, 4, arrived(s, 1)).then_inc(unit_used, 4)

                def ffn(f):
                    base = FFN_BASE[f]

                    def gate_up(g, u, more=0, rounds=0):
                        if g >= 2:
                            pe.wait_ge(z_free, layer * (2 * FT) + rounds + (FT * f + g - 1))
                        feature_major(Z[:, g % 2, 0:SEQ], u, more, arrived(2 * f, 1) if g == 0 else None)
                        feature_major(Z[:, g % 2, SEQ:2 * SEQ], u + 1, more)

                    def ready(g, rounds=0):
                        return h_ready, layer * (2 * FT) + rounds + (FT * f + g + 1)

                    def down_of(g, u, more=0, rounds=0, first=False):
                        pe.wait_ge(*ready(g, rounds))
                        down(hidden_of(g), u, first, more)

                    for t in range(TILES):
                        transposes(2 * f, t)
                    gate_up(0, base)
                    gate_up(1, base + 2)
                    down_of(0, base + 4, first=True)
                    with pe.Fori(0, (FT - 4) // 2) as j:
                        for g in range(2, 4):
                            gate_up(g, base + 3 * g - 1, j * RING, j * 2)
                            down_of(g - 1, base + 3 * g + 1, j * RING, j * 2)
                    end = base + FFN_UNITS
                    gate_up(FT - 2, end - 7)
                    gate_up(FT - 1, end - 5)
                    last = range(FT - HELD, FT)
                    down_last([hidden_of(g) for g in last], end - HELD, [ready(g) for g in last])

                def mixer():
                    base = MIX_BASE
                    pe.wait_ge(consts_ready, 2)
                    pre_and_first_units(1, base)
                    for q in range(2, NPAIR):
                        if q == 12:
                            pe.wait_ge(conv_in, layer + 1)
                        elif q == 13:
                            pe.wait_ge(mix_f, layer * 2 + 1)
                        else:
                            pe.wait_ge(z_evac, layer * 10 + q - 1)
                        name, _ = PAIRS[q]
                        if name == "av":
                            for t in range(TILES):
                                ins = token_major(Z[:, q % 2, t * SEQ:(t + 1) * SEQ], t, base + 2 * q, 2)
                            ins.then_inc(unit_used, 2)
                        else:
                            feature_major(Z[:, q % 2, 0:SEQ], base + 2 * q)
                            feature_major(Z[:, q % 2, SEQ:2 * SEQ], base + 2 * q + 1)
                        if q == FIRST_LEVEL_STEP + 1:
                            pe.wait_ge(z_evac, layer * 10 + 6)
                            pe.wait_ge(k_ready, layer + 1)
                            for i in range(8):
                                ins = pe.matmul(ACC[:, 2 + i // 4, i % 4 * P:(i % 4 + 1) * P],
                                                flat(K)[:, i * P:(i + 1) * P], flat(Q)[:, i * P:(i + 1) * P],
                                                start=True, stop=True)
                            ins.then_inc(own_ps, 1)
                        n = q - FIRST_LEVEL_STEP - 1
                        if 0 <= n <= NLV:
                            pe.wait_ge(level_in, layer * (NLV + 1) + n + 1)
                            if n >= 2:
                                pe.wait_ge(level_out, layer * (NLV + 1) + n - 1)
                            w = P // 2 if n < NLV else P
                            for i in range(HALF // w):
                                key = flat(KL)[:, i * P:(i + 1) * P] if n < NLV else KL[:, i, 0:P]
                                ins = pe.matmul(ACC[:, n % 2, i * w:(i + 1) * w], key, QL[:, i * w:(i + 1) * w],
                                                start=True, stop=True)
                            ins.then_inc(level_ps, 1)
                        if q == 8:
                            pe.wait_ge(z_evac, layer * 10 + 8)
                            pe.wait_ge(own_out, layer + 1)
                            for h in range(AT_HEADS):
                                pe.matmul(AUX[:, 0, h * P:(h + 1) * P], AQ[:, h // 2, 0:P], KZ[:, h, 0:P],
                                          start=True, stop=True)
                            for h in range(AT_HEADS):
                                ins = pe.matmul(ACC[:, 2 + h // 2, h % 2 * SEQ:(h % 2 + 1) * SEQ], AQ[:, h // 2, P:SEQ],
                                                KZ[:, h, :], start=True, stop=True)
                            ins.then_inc(qk_ps, 1)
                        if q == 11:
                            pe.wait_ge(pnorm, layer + 1)
                            for h in range(AT_HEADS):
                                pe.transpose(AUX[:, 0, h * P:(h + 1) * P], PA[:, h, :], ident[:, :])
                                for b in range(2):
                                    ins = pe.transpose(ACC[:, 2 + b, h * P:(h + 1) * P],
                                                       PB[:, h, b * P:(b + 1) * P], ident[:, :])
                            ins.then_inc(pT_ps, 1)
                        if q == 12:
                            pe.wait_ge(pT, layer * 2 + 2)
                            for h in range(AT_HEADS):
                                rows_ = slice(AT_DIM * (h % 2), AT_DIM * (h % 2) + AT_DIM)
                                to = AUX[rows_, 1, h // 2 * SEQ:(h // 2 + 1) * SEQ]
                                v = lambda b: AV[:, b, h * AT_DIM:(h + 1) * AT_DIM]
                                pe.matmul(to[:, 0:P], v(0), PTA[:, h, :], start=True, stop=True)
                                pe.matmul(to[:, P:SEQ], v(0), PTB[:, 0, h, :], start=True, stop=False)
                                ins = pe.matmul(to[:, P:SEQ], v(1), PTB[:, 1, h, :], start=False, stop=True)
                            ins.then_inc(at_ps, 1)
                    pe.wait_ge(level_out, layer * (NLV + 1) + NLV + 1)
                    pe.wait_ge(mix_lo, layer * 3 + 2)
                    pe.wait_ge(z_evac, layer * 10 + 9)
                    for h in range(HG_HEADS):
                        to = AUX[:, h // 2, h % 2 * SEQ:(h % 2 + 1) * SEQ]
                        v = lambda b: V[:, b, h * P:(h + 1) * P]
                        pe.matmul(to[:, 0:P], v(0), S[:, 2 * h, :], start=True, stop=True)
                        pe.matmul(to[:, P:SEQ], v(0), S10[:, h, :], start=True, stop=False)
                        ins = pe.matmul(to[:, P:SEQ], v(1), S[:, 2 * h + 1, :], start=False, stop=True)
                    ins.then_inc(o_ps, 1)
                    for o, kt in enumerate(OUT_ORDER):
                        if o == 1:
                            pe.wait_ge(o_sq, layer + 1)
                            pe.wait_ge(gate_done, layer * 2 + 2)
                            for a in range(2):
                                ins = pe.matmul(Z[:, a, :], ones[:, :], flat(D)[:, a * HALF:(a + 1) * HALF],
                                                start=True, stop=True)
                            ins.then_inc(ss_ps, 1)
                        if o % 2 == 0 and o <= 4:
                            pe.wait_ge(mix_lo, layer * 3 + o // 2 + 1)
                        if o < KT - HELD:
                            down(mixT[:, :, kt, :], base + 2 * NPAIR + o, o == 0)
                    down_last([mixT[:, :, kt, :] for kt in OUT_ORDER[-HELD:]], base + MIX_UNITS - HELD)

                ffn(0)
                mixer()
                ffn(1)



INPUTS = ["x", "norm_w", "ffn1_wg", "ffn1_wu", "ffn1_wd", "mix_w_in", "mix_w_out", "hg_lb", "hg_norm_w", "conv_w",
          "ffn2_wg", "ffn2_wu", "ffn2_wd", "rel_bias"]


def kernel(**inputs):
    import numpy as np
    import concourse.bacc as bacc
    from concourse.bass_utils import run_bass_kernel_spmd

    nc = bacc.Bacc("TRN2", target_bir_lowering=False, num_devices=1)
    f32 = mybir.dt.float32
    arrays = {f"in_{n}": np.ascontiguousarray(inputs[n]) for n in INPUTS}
    arrays["in_dist_onehot"] = np.array([[float(bucket(i - P) == b) for i in range(3 * P)]
                                         for b in range(BUCKETS)], np.float32)
    args = [nc.dram_tensor(n, a.shape, f32, kind="ExternalInput").ap() for n, a in arrays.items()]
    out = nc.dram_tensor("out_0", (1, SEQ, DM), f32, kind="ExternalOutput").ap()
    scratch = nc.dram_tensor("bias_scratch", (AT_HEADS, 3 * P), f32, kind="Internal").ap()
    trunk(nc, *args, out, scratch)
    r = run_bass_kernel_spmd(nc, [arrays], core_ids=[0])
    return r.results[0]["out_0"]
```
